# Optimizing a Trainium2 kernel written in Bass

```python
import jax, jax.numpy as jnp
from jax import lax
import numpy as np

D_MODEL = 2048
BATCH = 1
SEQ = 256
DEPTH = 1

HEAD_DIM = 128
N_HEADS_A = 8
N_HEADS_B = 8
D_A = N_HEADS_A * HEAD_DIM
D_B = N_HEADS_B * HEAD_DIM
D_MIX = D_A + D_B
IDX_HEADS = 16
IDX_DIM = 64
DSA_TOPK_MAX = 256
MOBA_BLOCK = 256
MOBA_TOPK_MAX = 3
DSA_Q_CHUNK = 64
MOBA_Q_CHUNK = 16
RMS_EPS = 1e-6
NEG_INF = -1e30

COL_WIDTHS = [D_A, D_A, D_A, D_A,
              IDX_HEADS * IDX_DIM, IDX_DIM, IDX_HEADS,
              D_B, D_B, D_B, D_B]
D_IN = sum(COL_WIDTHS)
COL_SPLITS = [int(s) for s in np.cumsum(COL_WIDTHS)[:-1]]


def _rms_norm(x, g):
    xf = x.astype(jnp.float32)
    y = xf * lax.rsqrt(jnp.mean(xf * xf, axis=-1, keepdims=True) + RMS_EPS)
    return (y * g.astype(jnp.float32)).astype(x.dtype)

def _alibi_slopes(n):
    return jnp.asarray(2.0 ** (-8.0 * np.arange(1, n + 1) / n), dtype=jnp.float32)

def _dsa_attention(q, k, v, q_idx, k_idx, w_idx, slopes):
    B, L, H, Dh = q.shape
    top_k = min(DSA_TOPK_MAX, L // 4)
    n_chunks = L // DSA_Q_CHUNK
    key_pos = jnp.arange(L)
    gather = jax.vmap(lambda t, i: t[i])

    def to_chunks(t):
        return jnp.swapaxes(t.reshape((B, n_chunks, DSA_Q_CHUNK) + t.shape[2:]), 0, 1)

    def chunk_fn(args):
        start, qc, qic, wc = args
        q_pos = start + jnp.arange(DSA_Q_CHUNK)
        logits = jnp.einsum('bqhd,bsd->bqhs', qic, k_idx).astype(jnp.float32) * IDX_DIM ** -0.5
        score = jnp.einsum('bqh,bqhs->bqs', wc.astype(jnp.float32), jax.nn.relu(logits)) * IDX_HEADS ** -0.5
        causal = key_pos[None, :] <= q_pos[:, None]
        score = jnp.where(causal[None], score, NEG_INF)
        _, sel = lax.top_k(score, top_k)
        valid = sel <= q_pos[None, :, None]
        k_sel = gather(k, sel)
        v_sel = gather(v, sel)
        s = jnp.einsum('bqhd,bqkhd->bqhk', qc, k_sel).astype(jnp.float32) * Dh ** -0.5
        dist = (q_pos[None, :, None] - sel).astype(jnp.float32)
        s = s - slopes[None, None, :, None] * dist[:, :, None, :]
        s = jnp.where(valid[:, :, None, :], s, NEG_INF)
        p = jax.nn.softmax(s, axis=-1).astype(v.dtype)
        return jnp.einsum('bqhk,bqkhd->bqhd', p, v_sel)

    starts = jnp.arange(n_chunks) * DSA_Q_CHUNK
    out = lax.map(chunk_fn, (starts, to_chunks(q), to_chunks(q_idx), to_chunks(w_idx)))
    return jnp.swapaxes(out, 0, 1).reshape(B, L, H, Dh)

def _moba_attention(q, k, v, slopes):
    B, L, H, Dh = q.shape
    nb = -(-L // MOBA_BLOCK)
    Lp = nb * MOBA_BLOCK
    pad = ((0, 0), (0, Lp - L), (0, 0), (0, 0))
    kp = jnp.pad(k, pad)
    vp = jnp.pad(v, pad)
    qp = jnp.pad(q, pad)
    scale = Dh ** -0.5
    offs = jnp.arange(MOBA_BLOCK)
    qb = qp.reshape(B, nb, MOBA_BLOCK, H, Dh)
    kb = kp.reshape(B, nb, MOBA_BLOCK, H, Dh)
    vb = vp.reshape(B, nb, MOBA_BLOCK, H, Dh)

    s_self = jnp.einsum('bnqhd,bnshd->bnhqs', qb, kb).astype(jnp.float32) * scale
    rel = offs[:, None] - offs[None, :]
    s_self = s_self - slopes[:, None, None] * rel.astype(jnp.float32)
    s_self = jnp.where(rel >= 0, s_self, NEG_INF)
    lse_self = jax.nn.logsumexp(s_self, axis=-1)
    p_self = jnp.exp(s_self - lse_self[..., None]).astype(v.dtype)
    o_self = jnp.einsum('bnhqs,bnshd->bnqhd', p_self, vb).reshape(B, Lp, H, Dh)[:, :L]
    lse_self = jnp.swapaxes(lse_self, 2, 3).reshape(B, Lp, H)[:, :L]

    top_k = min(MOBA_TOPK_MAX, nb - 1)
    if top_k == 0:
        return o_self.astype(q.dtype)

    k_mean = jnp.mean(kb.astype(jnp.float32), axis=2)
    gate = jnp.einsum('bthd,bnhd->bthn', q.astype(jnp.float32), k_mean)
    q_blk = jnp.arange(L) // MOBA_BLOCK
    past = jnp.arange(nb)[None, :] < q_blk[:, None]
    gate = jnp.where(past[None, :, None, :], gate, NEG_INF)
    _, sel = lax.top_k(gate, top_k)

    k_bh = jnp.transpose(kb, (0, 3, 1, 2, 4))
    v_bh = jnp.transpose(vb, (0, 3, 1, 2, 4))
    bi = jnp.arange(B)[:, None, None, None]
    hi = jnp.arange(H)[None, None, :, None]
    n_chunks = L // MOBA_Q_CHUNK

    def to_chunks(t):
        return jnp.swapaxes(t.reshape((B, n_chunks, MOBA_Q_CHUNK) + t.shape[2:]), 0, 1)

    def chunk_fn(args):
        start, qc, sc = args
        q_pos = start + jnp.arange(MOBA_Q_CHUNK)
        valid = sc < (q_pos // MOBA_BLOCK)[None, :, None, None]
        k_g = k_bh[bi, hi, sc]
        v_g = v_bh[bi, hi, sc]
        s = jnp.einsum('bqhd,bqhjsd->bqhjs', qc, k_g).astype(jnp.float32) * scale
        key_pos = sc[..., None] * MOBA_BLOCK + offs
        dist = (q_pos[None, :, None, None, None] - key_pos).astype(jnp.float32)
        s = s - slopes[None, None, :, None, None] * dist
        s = jnp.where(valid[..., None], s, NEG_INF)
        s = s.reshape(B, MOBA_Q_CHUNK, H, top_k * MOBA_BLOCK)
        lse = jax.nn.logsumexp(s, axis=-1)
        p = jnp.exp(s - lse[..., None]).astype(v.dtype).reshape(B, MOBA_Q_CHUNK, H, top_k, MOBA_BLOCK)
        o = jnp.einsum('bqhjs,bqhjsd->bqhd', p, v_g)
        return o, lse

    starts = jnp.arange(n_chunks) * MOBA_Q_CHUNK
    o_hist, lse_hist = lax.map(chunk_fn, (starts, to_chunks(q), to_chunks(sel)))
    o_hist = jnp.swapaxes(o_hist, 0, 1).reshape(B, L, H, Dh)
    lse_hist = jnp.swapaxes(lse_hist, 0, 1).reshape(B, L, H)

    lse = jnp.logaddexp(lse_self, lse_hist)
    w_self = jnp.exp(lse_self - lse)[..., None]
    w_hist = jnp.exp(lse_hist - lse)[..., None]
    return (o_self * w_self + o_hist * w_hist).astype(q.dtype)

def _hybrid_layer(x, c, w_ada, b_ada, g_norm, w_in, q_norm_a, k_norm_a, k_norm_idx,
                  q_norm_b, k_norm_b, w_out):
    B, L, _ = x.shape
    mod = jax.nn.silu(c) @ w_ada + b_ada
    shift, scale, gate = jnp.split(mod, 3, axis=-1)
    h = _rms_norm(x, g_norm) * (1.0 + scale[:, None, :]) + shift[:, None, :]

    proj = h @ w_in
    qa, ka, va, za, q_idx, k_idx, w_idx, qb, kb, vb, zb = jnp.split(proj, COL_SPLITS, axis=-1)

    heads_a = (B, L, N_HEADS_A, HEAD_DIM)
    heads_b = (B, L, N_HEADS_B, HEAD_DIM)
    qa = _rms_norm(qa.reshape(heads_a), q_norm_a)
    ka = _rms_norm(ka.reshape(heads_a), k_norm_a)
    va = va.reshape(heads_a)
    q_idx = q_idx.reshape(B, L, IDX_HEADS, IDX_DIM)
    k_idx = _rms_norm(k_idx, k_norm_idx)
    qb = _rms_norm(qb.reshape(heads_b), q_norm_b)
    kb = _rms_norm(kb.reshape(heads_b), k_norm_b)
    vb = vb.reshape(heads_b)

    ya = _dsa_attention(qa, ka, va, q_idx, k_idx, w_idx, _alibi_slopes(N_HEADS_A))
    yb = _moba_attention(qb, kb, vb, _alibi_slopes(N_HEADS_B))

    ya = ya.reshape(B, L, D_A) * jax.nn.silu(za)
    yb = yb.reshape(B, L, D_B) * jax.nn.silu(zb)
    y = jnp.concatenate([ya, yb], axis=-1) @ w_out
    return x + gate[:, None, :] * y

def first_inputs(seed: int = 0) -> dict:
    key = jax.random.key(seed)
    ks = jax.random.split(key, 12)
    nrm = jax.random.normal
    x = nrm(ks[0], (BATCH, SEQ, D_MODEL), jnp.float32)
    c = nrm(ks[1], (BATCH, D_MODEL), jnp.float32)
    w_ada = nrm(ks[2], (DEPTH, D_MODEL, 3 * D_MODEL), jnp.float32) * (0.5 * D_MODEL ** -0.5)
    b_ada = 0.01 * nrm(ks[3], (DEPTH, 3 * D_MODEL), jnp.float32)
    g_norm = 1.0 + 0.02 * nrm(ks[4], (DEPTH, D_MODEL), jnp.float32)
    w_in = nrm(ks[5], (DEPTH, D_MODEL, D_IN), jnp.float32) * D_MODEL ** -0.5
    q_norm_a = 1.0 + 0.02 * nrm(ks[6], (DEPTH, HEAD_DIM), jnp.float32)
    k_norm_a = 1.0 + 0.02 * nrm(ks[7], (DEPTH, HEAD_DIM), jnp.float32)
    k_norm_idx = 1.0 + 0.02 * nrm(ks[8], (DEPTH, IDX_DIM), jnp.float32)
    q_norm_b = 1.0 + 0.02 * nrm(ks[9], (DEPTH, HEAD_DIM), jnp.float32)
    k_norm_b = 1.0 + 0.02 * nrm(ks[10], (DEPTH, HEAD_DIM), jnp.float32)
    w_out = nrm(ks[11], (DEPTH, D_MIX, D_MODEL), jnp.float32) * D_MIX ** -0.5
    return {"x": x, "c": c, "w_ada": w_ada, "b_ada": b_ada, "g_norm": g_norm, "w_in": w_in,
            "q_norm_a": q_norm_a, "k_norm_a": k_norm_a, "k_norm_idx": k_norm_idx,
            "q_norm_b": q_norm_b, "k_norm_b": k_norm_b, "w_out": w_out}

def first_block(x, c, w_ada, b_ada, g_norm, w_in, q_norm_a, k_norm_a, k_norm_idx,
              q_norm_b, k_norm_b, w_out):
    for i in range(DEPTH):
        x = _hybrid_layer(x, c, w_ada[i], b_ada[i], g_norm[i], w_in[i], q_norm_a[i], k_norm_a[i],
                          k_norm_idx[i], q_norm_b[i], k_norm_b[i], w_out[i])
    return x


CHUNK = 64
N_META = 16
D_ATTN = D_MODEL // 2
ATTN_HEADS = D_ATTN // HEAD_DIM
POOL_WINDOWS = (2, 4, 8, 16)
N_POOL_GROUPS = len(POOL_WINDOWS)
D_POOL = D_MODEL // 2
POOL_GROUP_DIM = D_POOL // N_POOL_GROUPS
D_FF = 11 * D_MODEL // 4
CONV_WIDTH = 3
Q_BLOCK = 128
EPS = 1e-6

SPLIT_SIZES = (D_ATTN, D_ATTN, D_ATTN, ATTN_HEADS, D_POOL, D_MODEL, D_MODEL)
SPLIT_IDX = tuple(int(i) for i in np.cumsum(SPLIT_SIZES)[:-1])
D_IN_2 = sum(SPLIT_SIZES)
F_OFF = 3 * D_ATTN


def rmsnorm(x, g):
    xf = x.astype(jnp.float32)
    y = xf * lax.rsqrt(jnp.mean(xf * xf, axis=-1, keepdims=True) + EPS)
    return (y * g.astype(jnp.float32)).astype(x.dtype)

def forgetting_attention(q, k, v, logf):
    B, L, H, Dh = q.shape
    n_blocks = -(-L // Q_BLOCK)
    Lp = n_blocks * Q_BLOCK
    pad = ((0, 0), (0, Lp - L), (0, 0), (0, 0))
    q = jnp.pad(q, pad)
    k = jnp.pad(k, pad)
    v = jnp.pad(v, pad)
    logf = jnp.pad(logf, ((0, 0), (0, Lp - L), (0, 0)))
    c = jnp.cumsum(logf, axis=1)
    c = jnp.transpose(c, (0, 2, 1))
    scale = HEAD_DIM ** -0.5
    pos = jnp.arange(Lp)
    outs = []
    for i in range(n_blocks):
        q0, q1 = i * Q_BLOCK, (i + 1) * Q_BLOCK
        qb = q[:, q0:q1]
        kb = k[:, :q1]
        vb = v[:, :q1]
        s = jnp.einsum('bqhd,bkhd->bhqk', qb, kb).astype(jnp.float32) * scale
        bias = c[:, :, q0:q1, None] - c[:, :, None, :q1]
        mask = pos[q0:q1, None] >= pos[None, :q1]
        s = jnp.where(mask[None, None], s + bias, -jnp.inf)
        p = jax.nn.softmax(s, axis=-1).astype(vb.dtype)
        outs.append(jnp.einsum('bhqk,bkhd->bqhd', p, vb))
    o = jnp.concatenate(outs, axis=1)[:, :L]
    return o.reshape(B, L, H * Dh)

def multiscale_pool(u, pool_w, pool_scale):
    B, L, _ = u.shape
    uf = u.astype(jnp.float32).reshape(B, L, N_POOL_GROUPS, POOL_GROUP_DIM)
    csum = jnp.cumsum(uf, axis=1)
    pos = jnp.arange(L)
    outs = []
    for g, w in enumerate(POOL_WINDOWS):
        cg = csum[:, :, g]
        prev = jnp.pad(cg[:, :L - w], ((0, 0), (w, 0), (0, 0)))
        cnt = jnp.minimum(pos + 1, w).astype(jnp.float32)[None, :, None]
        outs.append((cg - prev) / cnt - uf[:, :, g])
    d = jnp.stack(outs, axis=2).astype(u.dtype)
    y = jnp.einsum('blgc,gcd->blgd', d, pool_w).reshape(B, L, D_POOL)
    return y * pool_scale

def mixer_block(h, w_in, b_in, w_attn_o, pool_w, pool_scale, w_pool_o, w_out):
    B, L, _ = h.shape
    z = h @ w_in + b_in
    q, k, v, f_logit, u, g_attn, g_pool = jnp.split(z, SPLIT_IDX, axis=-1)
    q = q.reshape(B, L, ATTN_HEADS, HEAD_DIM)
    k = k.reshape(B, L, ATTN_HEADS, HEAD_DIM)
    v = v.reshape(B, L, ATTN_HEADS, HEAD_DIM)
    logf = jax.nn.log_sigmoid(f_logit.astype(jnp.float32))
    attn = forgetting_attention(q, k, v, logf)
    pool = multiscale_pool(u, pool_w, pool_scale)
    m = jax.nn.sigmoid(g_attn) * (attn @ w_attn_o) + jax.nn.sigmoid(g_pool) * (pool @ w_pool_o)
    return m @ w_out

def causal_dwconv(a, conv_w, conv_b):
    L = a.shape[1]
    ap = jnp.pad(a, ((0, 0), (CONV_WIDTH - 1, 0), (0, 0)))
    out = conv_b
    for j in range(CONV_WIDTH):
        out = out + ap[:, j:j + L] * conv_w[j]
    return out

def conv_ffn(h, w_up, conv_w, conv_b, w_down):
    a = causal_dwconv(h @ w_up, conv_w, conv_b)
    gate, val = jnp.split(a, 2, axis=-1)
    return (jax.nn.gelu(gate, approximate=True) * val) @ w_down

def second_inputs(seed: int = 0) -> dict:
    key = jax.random.key(seed)
    ks = jax.random.split(key, 18)
    f32 = jnp.float32
    nrm = lambda k, shape, s: jax.random.normal(k, shape, f32) * s
    gain = lambda k, n: jnp.ones((DEPTH, n), f32) + nrm(k, (DEPTH, n), 0.02)
    b_in = nrm(ks[4], (DEPTH, D_IN_2), 0.02)
    f_bias = jax.random.uniform(ks[5], (DEPTH, ATTN_HEADS), f32, 1.0, 5.0)
    b_in = b_in.at[:, F_OFF:F_OFF + ATTN_HEADS].add(f_bias)
    return {
        'x': nrm(ks[0], (BATCH, SEQ, D_MODEL), 1.0),
        'meta_tokens': nrm(ks[1], (N_META, D_MODEL), 1.0),
        'mix_pre_g': gain(ks[2], D_MODEL),
        'w_in': nrm(ks[3], (DEPTH, D_MODEL, D_IN_2), D_MODEL ** -0.5),
        'b_in': b_in,
        'w_attn_o': nrm(ks[6], (DEPTH, D_ATTN, D_MODEL), D_ATTN ** -0.5),
        'pool_w': nrm(ks[7], (DEPTH, N_POOL_GROUPS, POOL_GROUP_DIM, POOL_GROUP_DIM), POOL_GROUP_DIM ** -0.5),
        'pool_scale': jnp.ones((DEPTH, D_POOL), f32) + nrm(ks[8], (DEPTH, D_POOL), 0.1),
        'w_pool_o': nrm(ks[9], (DEPTH, D_POOL, D_MODEL), D_POOL ** -0.5),
        'w_out': nrm(ks[10], (DEPTH, D_MODEL, D_MODEL), D_MODEL ** -0.5),
        'mix_post_g': gain(ks[11], D_MODEL),
        'ffn_pre_g': gain(ks[12], D_MODEL),
        'w_ffn_up': nrm(ks[13], (DEPTH, D_MODEL, 2 * D_FF), D_MODEL ** -0.5),
        'ffn_conv_w': nrm(ks[14], (DEPTH, CONV_WIDTH, 2 * D_FF), CONV_WIDTH ** -0.5),
        'ffn_conv_b': nrm(ks[15], (DEPTH, 2 * D_FF), 0.02),
        'w_ffn_down': nrm(ks[16], (DEPTH, D_FF, D_MODEL), D_FF ** -0.5),
        'ffn_post_g': gain(ks[17], D_MODEL),
    }

def second_block(x, meta_tokens, mix_pre_g, w_in, b_in, w_attn_o, pool_w, pool_scale, w_pool_o,
              w_out, mix_post_g, ffn_pre_g, w_ffn_up, ffn_conv_w, ffn_conv_b, w_ffn_down,
              ffn_post_g):
    B = x.shape[0]
    meta = jnp.broadcast_to(meta_tokens.astype(x.dtype)[None], (B, N_META, D_MODEL))
    r = jnp.concatenate([meta, x], axis=1)
    for l in range(DEPTH):
        h = rmsnorm(r, mix_pre_g[l])
        mix = mixer_block(h, w_in[l], b_in[l], w_attn_o[l], pool_w[l], pool_scale[l],
                          w_pool_o[l], w_out[l])
        r = r + rmsnorm(mix, mix_post_g[l])
        h = rmsnorm(r, ffn_pre_g[l])
        ff = conv_ffn(h, w_ffn_up[l], ffn_conv_w[l], ffn_conv_b[l], w_ffn_down[l])
        r = r + rmsnorm(ff, ffn_post_g[l])
    return r[:, N_META:]


def setup_inputs(seed=0):
    out = dict(first_inputs(seed))
    for name, value in second_inputs(seed + 1).items():
        if name != "x":
            out[name + "_2"] = value
    return out


def reference(
    x, c, w_ada, b_ada, g_norm, w_in, q_norm_a, k_norm_a, k_norm_idx, q_norm_b, k_norm_b, w_out,
    meta_tokens_2, mix_pre_g_2, w_in_2, b_in_2, w_attn_o_2, pool_w_2, pool_scale_2, w_pool_o_2,
    w_out_2, mix_post_g_2, ffn_pre_g_2, w_ffn_up_2, ffn_conv_w_2, ffn_conv_b_2, w_ffn_down_2,
    ffn_post_g_2,
):
    x = first_block(
        x, c, w_ada, b_ada, g_norm, w_in, q_norm_a, k_norm_a, k_norm_idx, q_norm_b, k_norm_b,
        w_out,
    )
    return second_block(
        x, meta_tokens_2, mix_pre_g_2, w_in_2, b_in_2, w_attn_o_2, pool_w_2, pool_scale_2,
        w_pool_o_2, w_out_2, mix_post_g_2, ffn_pre_g_2, w_ffn_up_2, ffn_conv_w_2, ffn_conv_b_2,
        w_ffn_down_2, ffn_post_g_2,
    )


_drawn_inputs = setup_inputs


def setup_inputs(seed=0):
    import zlib

    import numpy as np

    out = dict(_drawn_inputs(seed))
    spreads = {}
    factors = {'b_ada': 5.698,
     'g_norm': 4.213,
     'q_norm_a': 8.0,
     'k_norm_a': 8.0,
     'k_norm_idx': 5.832,
     'q_norm_b': 8.0,
     'k_norm_b': 8.0,
     'mix_pre_g_2': 3.045,
     'mix_post_g_2': 13.31,
     'ffn_pre_g_2': 9.49,
     'ffn_conv_b_2': 10.053,
     'ffn_post_g_2': 20.787}
    for name, (base, spread) in spreads.items():
        noise = np.random.default_rng([zlib.crc32(name.encode()), seed]).standard_normal(out[name].shape)
        drawn = base * np.exp(spread * noise) if base else spread * noise
        out[name] = __import__('jax').numpy.asarray(drawn.astype(out[name].dtype))
    for name, factor in factors.items():
        out[name] = (out[name] * factor).astype(out[name].dtype)
    return out
```

```python
import numpy as np
from contextlib import ExitStack

import concourse.bass as bass
from concourse import mybir

FP32 = mybir.dt.float32
F32R = mybir.dt.float32r
ALU = mybir.AluOpType
ACT = mybir.ActivationFunctionType
AX = mybir.AxisListType

P = 128
D = 2048
DC = D // P
SEQ = 256
META = 16
ROWS = META + SEQ
CONV = 3
LIVE0 = META - (CONV - 1)
LIVE = ROWS - LIVE0
HD = 128
HEADS = 8
IDX_HEADS = 16
IDX_DIM = 64
TOPK = min(256, SEQ // 4)
FF = 11 * D // 4
FC = FF // P
EPS = 1e-6
NEG = -1e30
SENTINEL = -3e38
IN1 = 4 * 1024 + IDX_HEADS * IDX_DIM + IDX_DIM + IDX_HEADS + 4 * 1024
IN2 = 3 * 1024 + HEADS + 1024 + 2 * D
SLOTS = 4
PIECE = 1024
PANEL = 512
POOL_WINDOWS = (2, 4, 8, 16)
TABLE_LN_EXP = 6
TABLE_EXP_TANH = 0

V1_C, V1_BADA, V1_G, V1_QA, V1_KA, V1_QB, V1_KB, V1_KI, V1_N = 0, 16, 64, 80, 81, 82, 83, 84, 85
V2_PRE, V2_POST, V2_FFN, V2_QKV, V2_F, V2_UG, V2_PS, V2_N = 0, 16, 32, 48, 72, 73, 113, 121
CT = 2 * FC


def ds(start, n):
    return bass.ds(start, n)


class Job:

    def __init__(self, name, n, J, src, rhs, N, kp=2, cols=512, banks=(0, 1, 2, 3)):
        self.name, self.n, self.J, self.src, self.rhs, self.N = name, n, J, src, rhs, N
        self.kp, self.cols, self.banks = kp, cols, banks
        self.width = kp * cols

    def place(self, c):
        self.raw0, self.hi0 = c["raw"], c["hi"]
        self.used0, self.ready0, self.free0 = list(c["used"]), list(c["ready"]), list(c["free"])
        c["raw"] += self.n * self.J // 4
        c["hi"] += self.n * self.J // 4
        for s in range(SLOTS):
            if self.name in ("pool_w", "down"):
                c["used"][s] += self.n * self.J // 4
            else:
                c["used"][s] += self.n * (self.J // 4 - (s == SLOTS - 1))
        for b in self.banks:
            if self.name == "pool_w":
                c["free"][b] += 2
            elif self.name != "down":
                c["ready"][b] += self.n
                c["free"][b] += self.n

    def turn(self, i, j):
        return i * (self.J // 4) + j // 4

    def normal(self, i, j):
        if self.name in ("pool_w", "down"):
            return self.turn(i, j)
        return i * (self.J // 4 - 1) + j // 4


def at_least(eng, sem, value):
    if isinstance(value, int) and value <= 0:
        return
    eng.wait_ge(sem, value)


class Chain:

    def __init__(self, eng, sem):
        self.eng, self.sem, self.n, self.turn, self.per = eng, sem, 0, 0, 0

    def step(self, ins, wait=True):
        ins.then_inc(self.sem, 1)
        self.n += 1
        if wait:
            self.wait()

    def wait(self):
        self.eng.wait_ge(self.sem, self.n + self.turn * self.per)

    def enter(self, turn, per):
        self.turn, self.per, self.start = turn, per, self.n

    def leave(self, trips):
        assert self.n - self.start == self.per, (self.n - self.start, self.per)
        self.n = self.start + trips * self.per
        self.turn, self.per = 0, 0


class Memory:
    pass


def memory(nc, ctx, A):
    M = Memory()
    M.nc, M.A = nc, A
    base = 16512
    at = {"o": base}

    def put(name, shape, dt=FP32, offset=None):
        size = int(np.prod(shape[1:])) * 4
        here = at["o"] if offset is None else offset
        t = nc.alloc_sbuf_tensor_at(name, list(shape), dt, offset=here)
        end = here + (size + 31) // 32 * 32
        if offset is None:
            at["o"] = end
        assert end <= nc.sbuf_usable_end, name
        M.end = end
        return t

    M.raw = [put(f"raw{s}", [P, PIECE]) for s in range(SLOTS)]
    M.hi = [put(f"w_hi{s}", [P, PIECE], F32R) for s in range(SLOTS)]
    M.lo = [put(f"w_lo{s}", [P, PIECE], F32R) for s in range(SLOTS)]
    M.rT = put("rT", [P, DC * ROWS])
    act_at = at["o"]
    M.act_hi = put("act_hi", [P, DC * ROWS], F32R)
    M.act_lo = put("act_lo", [P, DC * ROWS], F32R)
    M.ident = put("ident", [P, P])
    M.ones = put("ones", [P, ROWS])
    M.c1 = put("cols1", [P, V1_N])
    M.c2 = put("cols2", [P, V2_N])
    M.cc = put("conv_cols", [P, 4 * CT])
    M.gqk = put("gain_qk", [P, 8])
    M.qsc = put("scale_qkv", [P, 6])
    M.bqkv = put("bias_qkv", [P, 24])
    M.bgate = put("bias_gates", [P, 32])
    M.silu_c = put("silu_c", [P, DC])
    M.shift = put("shift", [P, DC])
    M.gs = put("gain_scaled", [P, DC])
    M.gate = put("gate", [P, DC])
    M.slopes = put("slopes", [P, HEADS])
    M.w_idx = put("w_idx_rows", [P, 2 * IDX_HEADS])
    M.nmax = put("neg_max", [P, 4])
    M.sums = put("sums", [P, 4])
    M.rinv = put("rinv", [P, 4])
    M.ss8 = put("sumsq_parts", [P, 8])
    M.rsf = put("final_stats", [P, 8])
    M.eps = put("eps_col", [P, 1])
    M.cq = put("c_q", [P, 24])
    q0 = at["o"]
    M.region = q0

    ada_at = q0
    M.ada_x = [put(f"ada_x{s}", [P, D], offset=ada_at + s * 8192) for s in range(2)]
    M.ya_hi = put("ya_hi", [P, 8 * SEQ], F32R, ada_at)
    M.ya_lo = put("ya_lo", [P, 8 * SEQ], F32R, ada_at + 8192)
    M.ada_acc = put("ada_acc", [P, D], offset=ada_at + 16384)
    s_at = ada_at + 24576
    M.store = put("store", [P, 7 * 8 * SEQ], offset=s_at)
    store = lambda n: s_at + n * 8192
    M.x_rows = put("x_rows", [P, 2 * D], offset=store(1))
    M.meta_rows = put("meta_rows", [META, D], offset=store(3))
    M.vec1 = put("vec1", [V1_N, P], offset=store(4))
    M.vec2 = put("vec2", [V2_N, P], offset=store(4) + 512)
    M.vecc = put("vec_conv", [CT, 4 * P], offset=store(4) + 1024)
    M.idx_score = put("idx_score", [P, 384], offset=store(5))
    M.work = put("select_work", [P, 384], offset=store(5) + 1536)
    M.max8 = put("max8", [P, 16], offset=store(5) + 3072)
    M.kst = put("k_idx_raw", [P, SEQ], offset=store(5) + 3584)
    M.knn = put("k_idx_normed", [IDX_DIM, SEQ], offset=store(5) + 4608)
    M.dup = put("dup64", [IDX_DIM, P], offset=store(5) + 5632)
    M.relu = put("relu_logits", [P, 2 * 384], offset=store(6))
    M.qi_st = put("q_idx_staged", [P, 2 * SEQ], offset=store(6) + 3072)
    x = s_at + 7 * 8192
    M.sq = put("squares", [P, 4 * SEQ], offset=x)
    M.rs = put("rstd", [P, 4 * SEQ], offset=x + 4096)
    M.q_st = put("q_staged", [P, 2 * SEQ], offset=x + 8192)
    M.v_st = put("v_staged", [P, 2 * SEQ], offset=x + 10240)
    M.v_rows = put("v_rows", [P, 2 * SEQ], offset=x + 12288)
    M.prob = put("prob", [P, 2 * 384], offset=x + 14336)
    M.probT = put("probT", [P, 2 * 384], offset=x + 17408)
    M.dist = put("dist", [P, 384], offset=x + 20480)
    M.dist_sel = put("dist_selected", [P, 384], offset=x + 22016)
    M.k_idx = put("k_idx_twice", [P, SEQ], offset=x + 23552)

    M.qkv = put("qkv", [P, 24 * ROWS], offset=q0)
    M.pool_a = put("pool_a", [P, 8 * ROWS], offset=q0 + 8 * ROWS * 4)
    M.pool_b = put("pool_b", [P, 8 * ROWS], offset=q0 + 16 * ROWS * 4)
    g_at = q0 + 24 * ROWS * 4
    M.u = put("u", [P, 8 * ROWS], offset=g_at)
    g_at += 8 * ROWS * 4
    M.G = put("gates", [P, 32 * LIVE], offset=g_at)
    x = g_at + 32 * LIVE * 4
    M.o_hi = put("o_hi", [P, 8 * LIVE], F32R, x)
    M.o_lo = put("o_lo", [P, 8 * LIVE], F32R, x + 8 * LIVE * 4)
    x += 16 * LIVE * 4 + 64
    x = (x + 31) // 32 * 32
    M.ssum = put("sumsq", [P, ROWS], offset=x)
    M.rs2 = put("rstd2", [P, ROWS], offset=x + 1088)
    M.tmp2 = put("rstd2_tmp", [P, ROWS], offset=x + 2176)
    y = x + 3264
    M.sqr = put("squares2", [P, 4 * ROWS], offset=y)
    M.ht = put("h_part", [P, 4 * ROWS], offset=y + 4352)
    z = y
    M.prob2 = put("prob2", [P, 688], offset=z)
    M.probT2 = put("probT2", [P, 3 * LIVE], offset=z + 2752)
    M.mask2 = put("mask2", [P, 688], offset=z + 5856)
    M.q_st2 = put("q_staged2", [P, LIVE + 2], offset=z + 8608)
    M.v_st2 = put("v_staged2", [P, ROWS], offset=z + 9664)
    M.v_rows2 = put("v_rows2", [P, 3 * P], offset=z + 10752)
    M.e8 = put("head_row", [HEADS, P], offset=z + 12288)
    M.fx = put("log_f", [HEADS, 2 * ROWS], offset=z + 12800)

    M.F = put("ffn_act", [P, FC * SEQ], offset=q0)
    x = q0 + FC * SEQ * 4
    M.r_rows = put("r_rows", [P, 2 * D], offset=x)
    M.g_row = put("post_gain_rows", [P, D], offset=x + 16384)
    M.d_hi = put("down_hi", [P, 4 * SEQ], F32R, x + 24576)
    M.d_lo = put("down_lo", [P, 4 * SEQ], F32R, x + 28672)
    x += 32768
    M.gt = put("conv_gate", [P, 4 * SEQ], offset=x)
    M.gg = put("gelu_gate", [P, 4 * SEQ], offset=x + 4096)
    M.vt = put("conv_val", [P, 4 * SEQ], offset=x + 8192)
    M.y = put("y_out", [P, 2 * D], offset=act_at)

    M.acc = [nc.alloc_psum_tensor(f"acc{m}", [P, 512], FP32) for m in range(4)]
    M.X = nc.alloc_psum_tensor("psum_x", [P, 1024], FP32)
    M.Y = nc.alloc_psum_tensor("psum_y", [P, 1024], FP32)

    def sem(name):
        return ctx.enter_context(nc.semaphore(name))

    M.vec_in = sem("vec_in")
    M.x_in = sem("x_in")
    M.consts = sem("consts")
    M.v1_t = sem("v1_t")
    M.cols = sem("cols")
    M.v2_t = sem("v2_t")
    M.silu_c_done = sem("silu_c_done")
    M.xt_ready = sem("xt_ready")
    M.xt_done = sem("xt_done")
    M.xsum = sem("xsum")
    M.ada_cols = sem("ada_cols")
    M.gate_cols = sem("gate_cols")
    M.gate_done = sem("gate_done")
    M.ss_ready = sem("ss_ready")
    M.y2_ready = sem("y2_ready")
    M.rs_ready = sem("rs_ready")
    M.norm_done = sem("norm_done")
    M.src_ready = sem("src_ready")
    M.ahi_ready = sem("ahi_ready")
    M.act_ready = sem("act_ready")
    M.kw_ready = sem("kw_ready")
    M.kd_ready = sem("kd_ready")
    M.kidx_ready = sem("kidx_ready")
    M.qi_ready = sem("qi_ready")
    M.il_ready = sem("il_ready")
    M.rl_ready = sem("rl_ready")
    M.rl_used = sem("rl_used")
    M.q_ready = sem("q_ready")
    M.v_ready = sem("v_ready")
    M.s_ready = sem("s_ready")
    M.vt_ready = sem("vt_ready")
    M.vr_ready = sem("vr_ready")
    M.nm_ready = sem("nm_ready")
    M.e_ready = sem("e_ready")
    M.p_ready = sem("p_ready")
    M.pt_ready = sem("pt_ready")
    M.pt_a = sem("pt_a")
    M.pt_d = sem("pt_d")
    M.o_ready = sem("o_ready")
    M.o_done = sem("o_done")
    M.r_upd = sem("r_upd")
    M.sq_done = sem("sq_done")
    M.ssum_done = sem("ssum_done")
    M.f_ln = sem("f_ln")
    M.c_ready = sem("c_ready")
    M.cq_t = sem("cq_t")
    M.cq_ready = sem("cq_ready")
    M.q2_ready = sem("q2_ready")
    M.s2_ready = sem("s2_ready")
    M.vt2_ready = sem("vt2_ready")
    M.vr2_ready = sem("vr2_ready")
    M.nm2_ready = sem("nm2_ready")
    M.e2_ready = sem("e2_ready")
    M.p2_ready = sem("p2_ready")
    M.pt2_ready = sem("pt2_ready")
    M.pt2_a = sem("pt2_a")
    M.pt2_d = sem("pt2_d")
    M.o2_ready = sem("o2_ready")
    M.o2_done = sem("o2_done")
    M.d_done = sem("d_done")
    M.m_sum = sem("m_sum")
    M.cv_ready = sem("cv_ready")
    M.gg_ready = sem("gg_ready")
    M.F_ready = sem("F_ready")
    M.rr_t = sem("rr_t")
    M.rr_done = sem("rr_done")
    M.g_in = sem("g_in")
    M.dh_ready = sem("dh_ready")
    M.dl_ready = sem("dl_ready")
    M.down_done = sem("down_done")
    M.fin_ss = sem("fin_ss")
    M.fin_v = sem("fin_v")
    M.fin_ls = sem("fin_ls")
    M.y_part = sem("y_part")
    M.stored = sem("stored")
    M.chain_v = sem("chain_v")
    M.chain_a = sem("chain_a")
    M.chain_p = sem("chain_p")
    M.score_zero = sem("score_zero")
    M.y_even = sem("y_even")
    M.v2_ready = sem("v2_ready")
    M.y_odd = sem("y_odd")
    M.masks_done = sem("masks_done")
    M.v_in = sem("v_in")
    M.raw_in = [sem(f"raw_in{s}") for s in range(4)]
    M.hi_ready = [sem(f"hi_ready{s}") for s in range(4)]
    M.lo_ready = [sem(f"lo_ready{s}") for s in range(4)]
    M.used = [sem(f"used{s}") for s in range(4)]
    M.acc_ready = [sem(f"acc_ready{s}") for s in range(4)]
    M.acc_free = [sem(f"acc_free{s}") for s in range(4)]
    M.ada_in = [sem(f"ada_in{n}") for n in range(2)]
    M.ada_used = [sem(f"ada_used{n}") for n in range(2)]

    def rows_of(w, kp):
        return w.rearrange("(j k p) c -> j p k c", k=kp, p=P)

    def act(k, c0=0, n=SEQ):
        return M.act_hi[:, ROWS * k + c0:ROWS * k + c0 + n], M.act_lo[:, ROWS * k + c0:ROWS * k + c0 + n]

    w_in, w_in2 = rows_of(A["w_in"], 2), rows_of(A["w_in_2"], 2)
    w_in_s, w_in2_s = rows_of(A["w_in"], 4), rows_of(A["w_in_2"], 4)
    w_out, w_out2, w_up = rows_of(A["w_out"], 2), rows_of(A["w_out_2"], 2), rows_of(A["w_ffn_up_2"], 2)
    w_ao, w_po = rows_of(A["w_attn_o_2"], 2), rows_of(A["w_pool_o_2"], 2)
    pool_w = A["pool_w_2"].rearrange("g (k p) c -> g p k c", p=P)
    down = A["w_ffn_down_2"].rearrange("(i k p) (h c) -> i k h p c", k=4, p=P, h=2)

    def cols(w, c0, first=0):
        return lambda i, j: w[first + j][:, :, ds(c0 + i * PANEL, PANEL)]

    qb0 = IN1 - 4096
    jobs = [
        Job("qidx0", 1, 8, cols(w_in, 4096), act, SEQ),
        Job("strip", 1, 4, lambda i, j: w_in_s[j][:, :, 5120:5248], act, SEQ, 4, 128, (3,)),
        Job("qidx1", 1, 8, cols(w_in, 4096 + PANEL), act, SEQ),
        Job("qk_a", 4, 8, cols(w_in, 0), act, SEQ),
        Job("v_a", 2, 8, cols(w_in, 2048), act, SEQ),
        Job("qk_b", 4, 8, cols(w_in, qb0), act, SEQ),
        Job("v_b", 2, 8, cols(w_in, qb0 + 2048), act, SEQ),
        Job("z_a", 2, 8, cols(w_in, 3072), act, SEQ),
        Job("z_b", 2, 8, cols(w_in, qb0 + 3072), act, SEQ),
        Job("out_a", 4, 4, cols(w_out, 0), lambda k: (M.ya_hi[:, SEQ * k:SEQ * k + SEQ],
                                                      M.ya_lo[:, SEQ * k:SEQ * k + SEQ]), SEQ),
        Job("out_b", 4, 4, cols(w_out, 0, 4), act, SEQ),
        Job("qkv2", 6, 8, cols(w_in2, 0), lambda k: act(k, 0, ROWS), ROWS),
        Job("f2", 1, 4, lambda i, j: w_in2_s[j][:, :, 3072:3200], lambda k: act(k, 0, ROWS), ROWS,
            4, 128, (3,)),
        Job("u2", 2, 8, cols(w_in2, 3072 + HEADS), lambda k: act(k, 0, ROWS), ROWS),
        Job("g2", 8, 8, cols(w_in2, 4096 + HEADS), lambda k: act(k, LIVE0, LIVE), LIVE),
        Job("attn_o", 4, 4, cols(w_ao, 0), lambda k: (M.o_hi[:, LIVE * k:LIVE * k + LIVE],
                                                      M.o_lo[:, LIVE * k:LIVE * k + LIVE]), LIVE),
        Job("pool_w", 1, 4, lambda i, j: pool_w[j], lambda k: act(k, 0, LIVE), LIVE, 2, 256),
        Job("pool_o", 4, 4, cols(w_po, 0), lambda k: act(8 + k, 0, LIVE), LIVE),
        Job("out2", 4, 8, cols(w_out2, 0), lambda k: act(k, 0, LIVE), LIVE),
        Job("up", 22, 8, None, lambda k: act(k, 0, LIVE), LIVE),
        Job("down", 11, 8, lambda i, j: down[i, j // 2, j % 2], None, 512, 1, 1024, ()),
    ]
    M.w_up = w_up
    M.mk, n = {}, 0
    for name, chunks in (("qidx0", 16), ("out_a", 8), ("out_b", 8), ("qkv2", 16), ("attn_o", 8),
                         ("pool_w", 8), ("pool_o", 8), ("out2", 16), ("up", 16)):
        M.mk[name] = n
        n += chunks
    counts = {"raw": 16, "hi": 0, "used": [0] * 4, "ready": [0] * 4, "free": [0] * 4}
    M.job = {}
    for job in jobs:
        job.place(counts)
        M.job[job.name] = job
    return M


def sp_program(M, sp):
    A, job = M.A, M.job

    def piece(dst, src, s, uses):
        at_least(sp, M.lo_ready[s], uses)
        sp.dma_start(dst, src).then_inc(M.raw_in[s], 16)

    def panel(job, i, after={}):
        for j in range(job.J):
            s = j % SLOTS
            src = job.src(i, j)
            dst = M.raw[s][:, 0:job.width]
            if len(src.shape) == 3:
                dst = dst.rearrange("p (k c) -> p k c", k=job.kp)
            piece(dst, src, s, job.raw0 + job.turn(i, j))
            for step in after.get(j, ()):
                step()

    for row, n, src in ((V1_C, 16, A["c"]), (V1_BADA, 48, A["b_ada"]), (V1_G, 16, A["g_norm"]),
                        (V1_QA, 1, A["q_norm_a"]), (V1_KA, 1, A["k_norm_a"]),
                        (V1_QB, 1, A["q_norm_b"]), (V1_KB, 1, A["k_norm_b"])):
        sp.dma_start(M.vec1[row:row + n, :], src.rearrange("a (r c) -> (a r) c", c=P)).then_inc(M.vec_in, 16)
    for half in range(2):
        sp.dma_start(M.vec1[V1_KI:V1_KI + 1, half * IDX_DIM:(half + 1) * IDX_DIM],
                     A["k_norm_idx"]).then_inc(M.vec_in, 16)

    w_ada = A["w_ada"].rearrange("(k p) (t h c) -> k t h p c", p=P, t=3, h=2)
    for t in range(2):
        def ada_rows(i, uses):
            for s in range(SLOTS):
                at_least(sp, M.lo_ready[s], uses)
                sp.dma_start(M.raw[s][:, :], w_ada[ds(2 * i + s // 2, 1), t, s % 2]
                             .rearrange("k p c -> p (k c)")).then_inc(M.raw_in[s], 16)

        ada_rows(0, t * (DC // 2))
        with sp.Fori(0, DC // 2 - 1) as i:
            ada_rows(i + 1, i + 1 + t * (DC // 2))

    gates = w_ada[:, 2].rearrange("k h p c -> k p h c")

    def gate_chunk(n):
        def go():
            at_least(sp, M.ada_used[n % 2], n // 2 if isinstance(n, int) else n)
            sp.dma_start(M.ada_x[n % 2][:, :].rearrange("p (h c) -> p h c", h=2), gates[n]
                         ).then_inc(M.ada_in[n % 2], 16)
        return go

    def gate_pair(turn):
        def go(b):
            def run():
                at_least(sp, M.ada_used[b], turn)
                sp.dma_start(M.ada_x[b][:, :].rearrange("p (h c) -> p h c", h=2),
                             gates[ds(2 * turn + b, 1)].rearrange("k p h c -> p (k h) c")
                             ).then_inc(M.ada_in[b], 16)
            return run
        return {3: [go(0)], 6: [go(1)]}

    panel(job["qidx0"], 0)
    panel(job["strip"], 0)
    panel(job["qidx1"], 0, gate_pair(0))
    with sp.Fori(0, job["qk_a"].n) as i:
        panel(job["qk_a"], i, gate_pair(i + 1))
    with sp.Fori(0, job["v_a"].n) as i:
        panel(job["v_a"], i)
    with sp.Fori(0, job["qk_b"].n) as i:
        panel(job["qk_b"], i)
    panel(job["v_b"], 0, {1: [gate_chunk(10)], 3: [gate_chunk(11)], 5: [gate_chunk(12)]})
    panel(job["v_b"], 1, {1: [gate_chunk(13)], 3: [gate_chunk(14)], 5: [gate_chunk(15)]})
    for name in ("z_a", "z_b", "out_a", "out_b", "qkv2"):
        with sp.Fori(0, job[name].n) as i:
            panel(job[name], i)
    panel(job["f2"], 0)
    for name in ("u2", "g2", "attn_o"):
        with sp.Fori(0, job[name].n) as i:
            panel(job[name], i)
    panel(job["pool_w"], 0)
    for name in ("pool_o", "out2"):
        with sp.Fori(0, job[name].n) as i:
            panel(job[name], i)
    up = job["up"]
    with sp.Fori(0, up.n // 2) as i:
        for part in range(2):
            for j in range(up.J):
                s = j % SLOTS
                piece(M.raw[s][:, :].rearrange("p (k c) -> p k c", k=2),
                      M.w_up[j][:, :, ds(part * FF + i * PANEL, PANEL)], s,
                      up.raw0 + up.turn(2 * i + part, j))
    sp.wait_ge(M.cv_ready, 4)
    sp.dma_start(M.g_row[:, :], A["ffn_post_g_2"].broadcast_to((P, D))).then_inc(M.g_in, 16)
    down = job["down"]
    with sp.Fori(0, down.n) as i:
        for j in range(down.J):
            s = j % SLOTS
            piece(M.raw[s][:, :], A["w_ffn_down_2"].rearrange("(i k p) (h c) -> i k h p c", k=4, p=P, h=2)
                  [ds(i, 1), j // 2, j % 2].rearrange("i p c -> p (i c)"), s, down.raw0 + down.turn(i, j))
    out = A["out"].rearrange("a (t p) d -> p (a t) d", p=P)
    y = M.y[:, :].rearrange("p (t d) -> p t d", t=2)
    for n in range(8):
        t, c = n // 4, n % 4
        sp.wait_ge(M.y_even if n % 2 == 0 else M.y_odd, n // 2 + 1)
        sp.dma_start(out[:, t, c * PANEL:(c + 1) * PANEL], y[:, t, c * PANEL:(c + 1) * PANEL]
                     ).then_inc(M.stored, 16)
    sp.wait_ge(M.stored, 8 * 16)


def pool_program(M, pool):
    job = M.job
    ch = Chain(pool, M.chain_p)
    ch.step(pool.memset(M.ident[:, :], 0.0))
    ch.step(pool.affine_select(out=M.ident[:, :], in_=M.ident[:, :], compare_op=ALU.not_equal, fill=1.0,
                               base=0, pattern=[[-1, P]], channel_multiplier=1))
    pool.memset(M.ones[:, :], 1.0)
    for h in range(HEADS):
        pool.memset(M.slopes[:, h:h + 1], 2.0 ** (-8.0 * (h + 1) / HEADS))
    pool.memset(M.eps[:, :], EPS)
    pool.memset(M.ada_acc[:, :], 0.0)
    for t in range(2):
        part = M.dist[:, t * P:t * P + (t + 1) * P]
        n = (t + 1) * P
        ch.step(pool.iota(part, pattern=[[1, n]], base=-t * P, channel_multiplier=-1,
                          allow_small_or_imprecise_dtypes=True))
        ch.step(pool.affine_select(out=part, in_=part, compare_op=ALU.is_ge, fill=NEG,
                                   base=t * P, pattern=[[-1, n]], channel_multiplier=1))
    pool.memset(M.qsc[:, 0:2], HD ** -0.5)
    pool.memset(M.qsc[:, 2:6], 1.0)
    pool.memset(M.sums[:, :], 1.0).then_inc(M.consts, 1)

    def stage_idx(u):
        pool.wait_ge(M.acc_free[3], job["qidx1"].free0[3] + 1)
        at_least(pool, M.il_ready, 2 * u)
        pool.tensor_copy(M.qi_st[:, :], M.store[:, ds(u * 512, 512)]).then_inc(M.qi_ready, 1)

    ch.step(pool.memset(M.dup[:, :], 0.0))
    for half in range(2):
        part = M.dup[:, half * IDX_DIM:(half + 1) * IDX_DIM]
        ch.step(pool.affine_select(out=part, in_=part, compare_op=ALU.not_equal, fill=1.0, base=0,
                                   pattern=[[-1, IDX_DIM]], channel_multiplier=1))
    pool.memset(M.idx_score[:, :], 0.0).then_inc(M.score_zero, 1)
    stage_idx(0)
    with pool.Fori(0, 3) as i:
        stage_idx(i + 1)

    def stage(u, q_at, v_at, norms, v_free):
        pool.wait_ge(M.norm_done, norms)
        at_least(pool, M.s_ready, u)
        pool.tensor_copy(M.q_st[:, :], M.store[:, q_at]).then_inc(M.q_ready, 1)
        pool.wait_ge(M.acc_free[3], v_free)
        at_least(pool, M.vt_ready, u)
        pool.tensor_copy(M.v_st[:, :], M.store[:, v_at]).then_inc(M.v_ready, 1)

    for turn, (q_tile, v_tile, vjob) in enumerate(((8, 24, "v_a"), (32, 48, "v_b"))):
        vfree = job[vjob].free0[3] + job[vjob].n
        stage(4 * turn, ds(q_tile * SEQ, 512), ds(v_tile * SEQ, 512), 5 + 4 * turn, vfree)
        with pool.Fori(0, 3) as i:
            stage(i + 4 * turn + 1, ds(q_tile * SEQ + i * 512 + 512, 512),
                  ds(v_tile * SEQ + i * 512 + 512, 512), 5 + 4 * turn, vfree)

    def sum_squares(base, first=0):
        with pool.Fori(0, 4) as i:
            for b in range(4):
                pool.wait_ge(M.sq_done, base + 4 * i + b + 1)
                pool.wait_ge(M.ssum_done, base // 16 + base + 4 * i + b + 1)
                pool.tensor_tensor(M.ssum[:, first:ROWS], M.ssum[:, first:ROWS],
                                   M.sqr[:, b * ROWS + first:(b + 1) * ROWS], ALU.add).then_inc(M.ssum_done, 1)

    pool.wait_ge(M.act_ready, M.mk["qkv2"])
    pool.memset(M.ssum[:, :], 0.0).then_inc(M.ssum_done, 1)
    sum_squares(0)

    pool.wait_ge(M.act_ready, M.mk["qkv2"] + 16)
    for t, (c0, n, rows) in enumerate(((0, 144, P), (144, ROWS, P), (416, ROWS, 2))):
        part = M.mask2[0:rows, c0:c0 + n]
        ch.step(pool.memset(part, 0.0))
        ch.step(pool.affine_select(out=part, in_=part, compare_op=ALU.is_ge, fill=NEG,
                                   base=LIVE0 + t * P, pattern=[[-1, n]], channel_multiplier=1),
                wait=False)
    ch.wait()
    pool.memset(M.v_rows2[:, :], 0.0).then_inc(M.masks_done, 1)

    def stage2(h):
        at_least(pool, M.s2_ready, h)
        pool.wait_ge(M.acc_free[3], job["qkv2"].free0[3] + 6)
        pool.tensor_copy(M.e8[:, :], M.ident[0:HEADS, ds(h, 1)].broadcast_to((HEADS, P)))
        pool.tensor_copy(M.q_st2[:, 0:LIVE], M.qkv[:, ds(h * ROWS + LIVE0, LIVE)]).then_inc(M.q2_ready, 1)
        at_least(pool, M.vt2_ready, h)
        pool.tensor_copy(M.v_st2[:, :], M.qkv[:, ds((16 + h) * ROWS, ROWS)]).then_inc(M.v2_ready, 1)

    stage2(0)
    with pool.Fori(0, HEADS - 1) as i:
        stage2(i + 1)

    u = M.u[:, :].rearrange("p (g t) -> p g t", g=8)
    a = M.pool_a[:, :].rearrange("p (g t) -> p g t", g=8)
    b = M.pool_b[:, :].rearrange("p (g t) -> p g t", g=8)
    pool.wait_ge(M.o2_ready, HEADS)
    src, dst, shift = u, a, 1
    for g in range(4):
        lo = 0 if g == 0 else 2
        if g == 0:
            pool.tensor_copy(dst[:, :, 0:1], u[:, :, 0:1])
            ch.step(pool.tensor_tensor(dst[:, :, 1:ROWS], u[:, :, 1:ROWS], u[:, :, 0:ROWS - 1], ALU.add))
        else:
            first = 2 ** (g + 1) - 2
            ch.step(pool.tensor_tensor(dst[:, 2 * g:8, first:ROWS], src[:, 2 * g:8, first:ROWS],
                                       src[:, 2 * g:8, first - shift:ROWS - shift], ALU.add))
        w = POOL_WINDOWS[g]
        part = dst[:, 2 * g:2 * g + 2, LIVE0:ROWS]
        if w > LIVE0 + 1:
            ch.step(pool.tensor_scalar(dst[:, 2 * g:2 * g + 2, LIVE0:LIVE0 + 1],
                                       dst[:, 2 * g:2 * g + 2, LIVE0:LIVE0 + 1],
                                       float(w) / (LIVE0 + 1), 0.0, ALU.mult, ALU.add))
        ch.step(pool.tensor_scalar(part, part, 1.0 / w, 0.0, ALU.mult, ALU.add))
        ins = pool.tensor_tensor(u[:, 2 * g:2 * g + 2, LIVE0:ROWS], part,
                                 u[:, 2 * g:2 * g + 2, LIVE0:ROWS], ALU.subtract)
        ins.then_inc(M.d_done, 1)
        src, dst = dst, (b if dst is a else a)
        shift = 2 ** (g + 1)

    with pool.Fori(0, 4) as i:
        for m in range(4):
            pool.wait_ge(M.acc_free[m], job["pool_o"].free0[m] + i + 1)
            part = M.G[:, ds((4 * i + m) * LIVE, LIVE)]
            pool.tensor_tensor(part, part, M.G[:, ds((16 + 4 * i + m) * LIVE, LIVE)], ALU.add
                               ).then_inc(M.m_sum, 1)
    pool.memset(M.ssum[:, :], 0.0).then_inc(M.ssum_done, 1)
    sum_squares(16, LIVE0)

    with pool.Fori(0, 11) as i:
        pool.wait_ge(M.gg_ready, i + 1)
        pool.wait_ge(M.acc_free[3], job["up"].free0[3] + 2 * i + 2)
        pool.tensor_tensor(M.F[:, ds(i * 4 * SEQ, 4 * SEQ)], M.gg[:, :], M.vt[:, :], ALU.mult
                           ).then_inc(M.F_ready, 1)
    for n in range(1, 8, 2):
        pool.wait_ge(M.y_part, n + 1)
        pool.tensor_tensor(M.y[:, n * 512:(n + 1) * 512], M.y[:, n * 512:(n + 1) * 512],
                           M.r_rows[:, n * 512:(n + 1) * 512], ALU.add).then_inc(M.y_odd, 1)


def pe_program(M, pe):
    job = M.job
    ones, ident = M.ones, M.ident
    store = M.store

    def panel(job, i, after={}, acts=None, hook_at_end=()):
        for j in range(job.J):
            s = j % SLOTS
            pe.wait_ge(M.lo_ready[s], job.raw0 + job.turn(i, j) + 1)
            if acts is not None:
                pe.wait_ge(M.act_ready, acts + job.kp * (j + 1))
            for b in job.banks:
                col = 0 if len(job.banks) == 1 else b * P
                out = M.acc[b][:, 0:job.N]
                if j == 0:
                    at_least(pe, M.acc_free[b], job.free0[b] + i)
                for k in range(job.kp):
                    c = job.kp * j + k
                    last = c == job.kp * job.J - 1
                    a_hi, a_lo = job.rhs(c)
                    w_hi = M.hi[s][:, k * job.cols + col:k * job.cols + col + P]
                    w_lo = M.lo[s][:, k * job.cols + col:k * job.cols + col + P]
                    pe.matmul(out, w_lo, a_hi, start=c == 0, stop=False)
                    pe.matmul(out, w_hi, a_lo, start=False, stop=False)
                    ins = pe.matmul(out, w_hi, a_hi, start=False, stop=last)
                if j == job.J - 1:
                    ins.then_inc(M.acc_ready[b], 1)
            if j < job.J - 1:
                ins.then_inc(M.used[s], 1)
            for step in after.get(j, ()):
                step()

    def transpose(out, src, rows=P):
        return pe.transpose(out, src, ident[0:rows, 0:rows])

    pe.wait_ge(M.consts, 1)
    pe.wait_ge(M.vec_in, 9 * 16)
    transpose(M.Y[:, 0:V1_N], M.vec1[:, :], V1_N).then_inc(M.v1_t, 1)
    pe.wait_ge(M.x_in, 3 * 16)
    for k in range(DC):
        out = M.acc[k % 4]
        if k >= 4:
            pe.wait_ge(M.xt_done, k - 3)
        transpose(out[:, 0:META], M.meta_rows[:, k * P:(k + 1) * P], META)
        for t in range(2):
            ins = transpose(out[:, META + t * P:META + (t + 1) * P], M.x_rows[:, t * D + k * P:t * D + (k + 1) * P])
        ins.then_inc(M.xt_ready, 1)
        if k >= 2:
            sum_x(M, pe, k - 2)
    sum_x(M, pe, DC - 2)
    sum_x(M, pe, DC - 1)
    pe.wait_ge(M.vec_in, 9 * 16)
    pe.wait_ge(M.v_in, 11 * 16)
    transpose(M.Y[:, 512:512 + V2_N], M.vec2[:, :], V2_N)
    for t in range(3):
        transpose(M.Y[:, 640 + t * CT:640 + (t + 1) * CT], M.vecc[:, t * P:(t + 1) * P], CT)
    pe.wait_ge(M.cols, 1)
    transpose(M.Y[:, 128:128 + CT], M.vecc[:, 3 * P:4 * P], CT).then_inc(M.v2_t, 1)

    for t in range(2):
        for s in (2, 3):
            pe.wait_ge(M.lo_ready[s], (t + 1) * DC // 2)
        for m in range(DC):
            ins = pe.matmul(M.X[:, t * DC + m:t * DC + m + 1], M.ada_acc[:, m * P:(m + 1) * P],
                            ones[:, 0:1], start=True, stop=True)
        ins.then_inc(M.ada_cols, 1)

    panel(job["qidx0"], 0, acts=M.mk["qidx0"])
    panel(job["strip"], 0)

    def k_idx_sums():
        pe.wait_ge(M.acc_free[3], job["strip"].free0[3] + 1)
        pe.matmul(M.Y[0:IDX_DIM, 0:SEQ], ones[0:IDX_DIM, 0:IDX_DIM], M.sq[0:IDX_DIM, 0:SEQ],
                  start=True, stop=True).then_inc(M.ss_ready, 1)
        for t in range(2):
            ins = transpose(M.X[:, t * P:(t + 1) * P], M.kst[:, t * P:(t + 1) * P])
        ins.then_inc(M.kw_ready, 1)

    def k_idx_twice():
        pe.wait_ge(M.norm_done, 1)
        pe.wait_ge(M.score_zero, 1)
        pe.matmul(M.X[:, 512:512 + SEQ], M.dup[:, :], M.knn[:, :], start=True, stop=True
                  ).then_inc(M.kd_ready, 1)

    panel(job["qidx1"], 0, {0: [k_idx_sums], 5: [k_idx_twice]})

    def qk_sums(stored):
        def go():
            pe.wait_ge(M.acc_free[3], stored)
            for t in range(2):
                ins = pe.matmul(M.Y[:, t * 512:(t + 1) * 512], ones[:, 0:P], M.sq[:, t * 512:(t + 1) * 512],
                                start=True, stop=True)
            ins.then_inc(M.ss_ready, 1)
        return go

    def logits(u, tile):
        def go():
            n = 2 * u + tile
            if tile == 0:
                pe.wait_ge(M.qi_ready, u + 1)
            if isinstance(n, int) and n == 0:
                pe.wait_ge(M.kidx_ready, 1)
            else:
                pe.wait_ge(M.rl_ready, n)
            for half in range(2):
                parts = slice(half * IDX_DIM, (half + 1) * IDX_DIM)
                for t in range(2):
                    ins = pe.matmul(M.X[:, half * 512 + t * P:half * 512 + t * P + (t + 1) * P],
                                    M.qi_st[parts, tile * SEQ + t * P:tile * SEQ + (t + 1) * P],
                                    M.k_idx[parts, 0:(t + 1) * P], start=True, stop=True)
            ins.then_inc(M.il_ready, 1)
        return go

    a = job["qk_a"]
    panel(a, 0, {0: [logits(0, 0)], 3: [logits(0, 1)]})
    with pe.Fori(0, a.n - 1) as i:
        panel(a, i + 1, {0: [qk_sums(a.free0[3] + i + 1), logits(i + 1, 0)], 3: [logits(i + 1, 1)]})
    panel(job["v_a"], 0, {0: [qk_sums(a.free0[3] + 4)]})
    panel(job["v_a"], 1)

    def unit(u, k_off, norms):
        def score():
            pe.wait_ge(M.q_ready, u + 1)
            if isinstance(u, int) and u == 0:
                pe.wait_ge(M.rl_ready, 8)
            else:
                pe.wait_ge(M.pt_a, u)
                pe.wait_ge(M.pt_d, u)
            for h in range(2):
                for t in range(2):
                    ins = pe.matmul(M.X[:, h * 512 + t * P:h * 512 + t * P + (t + 1) * P],
                                    M.q_st[:, h * SEQ + t * P:h * SEQ + (t + 1) * P],
                                    M.store[:, ds(k_off + h * SEQ, (t + 1) * P)], start=True, stop=True)
            ins.then_inc(M.s_ready, 1)

        def v_rows():
            pe.wait_ge(M.v_ready, u + 1)
            pe.wait_ge(M.rs_ready, norms)
            at_least(pe, M.vr_ready, u)
            for h in range(2):
                for t in range(2):
                    ins = transpose(M.Y[:, t * 256 + h * P:t * 256 + (h + 1) * P],
                                    M.v_st[:, h * SEQ + t * P:h * SEQ + (t + 1) * P])
            ins.then_inc(M.vt_ready, 1)

        def probs_t():
            pe.wait_ge(M.p_ready, u + 1)
            for h in range(2):
                for blk in range(3):
                    ins = transpose(M.X[:, h * 512 + blk * P:h * 512 + (blk + 1) * P],
                                    M.prob[:, h * 384 + blk * P:h * 384 + (blk + 1) * P])
            ins.then_inc(M.pt_ready, 1)

        def values():
            pe.wait_ge(M.pt_a, u + 1)
            pe.wait_ge(M.pt_d, u + 1)
            pe.wait_ge(M.vr_ready, u + 1)
            at_least(pe, M.o_done, u)
            for h in range(2):
                out = M.Y[:, 512 + h * SEQ:512 + (h + 1) * SEQ]
                pe.matmul(out, M.v_rows[:, h * P:(h + 1) * P], M.probT[:, h * 384:h * 384 + SEQ],
                          start=True, stop=False)
                ins = pe.matmul(M.Y[:, 512 + h * SEQ + P:512 + (h + 1) * SEQ],
                                M.v_rows[:, 256 + h * P:256 + (h + 1) * P],
                                M.probT[:, h * 384 + SEQ:h * 384 + 384], start=False, stop=True)
            ins.then_inc(M.o_ready, 1)

        return score, v_rows, probs_t, values

    def hooks(u, k_off, norms, sums=()):
        score, v_rows, probs_t, values = unit(u, k_off, norms)
        return {0: [*sums, score], 2: [v_rows], 3: [probs_t], 5: [values]}

    b = job["qk_b"]
    k_a, k_b = 16 * SEQ, 40 * SEQ
    panel(b, 0, hooks(0, k_a, 6))
    with pe.Fori(0, b.n - 1) as i:
        panel(b, i + 1, hooks(i + 1, k_a + (i + 1) * 512, i + 7, (qk_sums(b.free0[3] + i + 1),)))
    panel(job["v_b"], 0, {0: [qk_sums(b.free0[3] + 4)]})
    panel(job["v_b"], 1)

    def gate_cols():
        pe.wait_ge(M.ada_used[1], DC // 2)
        pe.wait_ge(M.o_done, 4)
        for m in range(DC):
            ins = pe.matmul(M.Y[:, 512 + m:513 + m], M.ada_acc[:, m * P:(m + 1) * P], ones[:, 0:1],
                            start=True, stop=True)
        ins.then_inc(M.gate_cols, 1)

    for n, name in enumerate(("z_a", "z_b")):
        for i in range(2):
            u = 4 + 2 * n + i
            h = hooks(u, k_b + (u - 4) * 512, 10)
            if u == 4:
                h[0] = h[0] + [gate_cols]
                values = h[5][0]

                def after_gate():
                    pe.wait_ge(M.gate_done, 1)
                    values()
                h[5] = [after_gate]
            panel(job[name], i, h)

    for name in ("out_a", "out_b"):
        o = job[name]
        panel(o, 0, acts=M.mk[name])
        with pe.Fori(0, o.n - 1) as i:
            panel(o, i + 1)

    def live_sums(count):
        pe.wait_ge(M.ssum_done, count)
        pe.matmul(M.X[:, 0:ROWS], ones[:, 0:P], M.ssum[:, :], start=True, stop=True
                  ).then_inc(M.ss_ready, 1)

    live_sums(17)
    q = job["qkv2"]
    panel(q, 0, acts=M.mk["qkv2"])
    with pe.Fori(0, q.n - 1) as i:
        panel(q, i + 1)
    panel(job["f2"], 0)
    panel(job["u2"], 0)

    def c_rows():
        pe.wait_ge(M.c_ready, 1)
        for t, n in enumerate((P, P, 2)):
            ins = pe.transpose(M.X[0:n, 8 * t:8 * t + 8], M.fx[:, ROWS + LIVE0 + t * P:ROWS + LIVE0 + t * P + n],
                               ident[0:HEADS, 0:HEADS])
        ins.then_inc(M.cq_t, 1)

    panel(job["u2"], 1, {3: [c_rows]})

    def unit2(h, k_off):
        tiles = ((0, 144, P), (144, ROWS, P), (512, ROWS, 2))

        def score():
            pe.wait_ge(M.q2_ready, h + 1)
            if isinstance(h, int) and h == 0:
                pe.wait_ge(M.cq_ready, 1)
            else:
                pe.wait_ge(M.pt2_a, h)
                pe.wait_ge(M.pt2_d, h)
            for t, (c0, n, rows) in enumerate(tiles):
                out = M.X[0:rows, c0:c0 + n]
                pe.matmul(out, M.q_st2[:, t * P:t * P + rows], M.qkv[:, ds(k_off, n)], start=True, stop=False)
                ins = pe.matmul(out, M.e8[:, 0:rows], M.fx[:, ROWS:ROWS + n], start=False, stop=True)
            ins.then_inc(M.s2_ready, 1)

        def v_rows():
            pe.wait_ge(M.v2_ready, h + 1)
            at_least(pe, M.vr2_ready, h)
            for t in range(2):
                transpose(M.Y[:, t * P:(t + 1) * P], M.v_st2[:, t * P:(t + 1) * P])
            transpose(M.Y[0:META, 2 * P:3 * P], M.v_st2[:, 2 * P:ROWS]).then_inc(M.vt2_ready, 1)

        def probs_t():
            pe.wait_ge(M.p2_ready, h + 1)
            pr = M.prob2
            transpose(M.X[:, 0:P], pr[:, 0:P])
            transpose(M.X[:, P:2 * P], pr[:, 144:144 + P])
            transpose(M.X[:, 2 * P:LIVE], pr[0:2, 416:416 + P], 2)
            transpose(M.X[0:16, LIVE:LIVE + P], pr[:, 144 + 256:144 + 272])
            transpose(M.X[0:16, LIVE + P:LIVE + P + 2], pr[0:2, 416 + 256:416 + 272], 2)
            transpose(M.X[0:16, 512:512 + P], pr[:, P:144])
            transpose(M.X[:, 512 + P:512 + 2 * P], pr[:, 144 + P:144 + 2 * P])
            transpose(M.X[:, 512 + 2 * P:512 + LIVE], pr[0:2, 416 + P:416 + 2 * P], 2).then_inc(M.pt2_ready, 1)

        def values():
            pe.wait_ge(M.pt2_a, h + 1)
            pe.wait_ge(M.pt2_d, h + 1)
            pe.wait_ge(M.vr2_ready, h + 1)
            at_least(pe, M.o2_done, h)
            vr, pt = M.v_rows2, M.probT2
            z = 512
            pe.matmul(M.Y[:, z:z + LIVE], vr[:, 0:P], pt[:, 0:LIVE], start=True, stop=False)
            pe.matmul(M.Y[:, z:z + P], vr[0:16, P:2 * P], pt[0:16, LIVE:LIVE + P], start=False, stop=False)
            pe.matmul(M.Y[:, z + P:z + LIVE], vr[:, P:2 * P], pt[:, LIVE + P:2 * LIVE], start=False, stop=False)
            pe.matmul(M.Y[:, z + P:z + LIVE], vr[0:16, 2 * P:3 * P], pt[0:16, 2 * LIVE:2 * LIVE + 130],
                      start=False, stop=True).then_inc(M.o2_ready, 1)

        return {0: [score], 1: [v_rows], 3: [probs_t], 5: [values]}

    g = job["g2"]
    panel(g, 0, unit2(0, 8 * ROWS))
    with pe.Fori(0, g.n - 1) as i:
        panel(g, i + 1, unit2(i + 1, (i + 9) * ROWS))

    o = job["attn_o"]
    panel(o, 0, acts=M.mk["attn_o"])
    with pe.Fori(0, o.n - 1) as i:
        panel(o, i + 1)

    w = job["pool_w"]
    for j in range(4):
        pe.wait_ge(M.lo_ready[j], w.raw0 + 1)
        pe.wait_ge(M.act_ready, M.mk["pool_w"] + 2 * (j + 1))
        for e in range(2):
            b_ = (2 * j + e) % 4
            pe.wait_ge(M.acc_free[b_], w.free0[b_] + j // 2)
            for k in range(2):
                a_hi, a_lo = w.rhs(2 * j + k)
                w_hi = M.hi[j][:, k * 256 + e * P:k * 256 + (e + 1) * P]
                w_lo = M.lo[j][:, k * 256 + e * P:k * 256 + (e + 1) * P]
                out = M.acc[b_][:, 0:LIVE]
                pe.matmul(out, w_lo, a_hi, start=k == 0, stop=False)
                pe.matmul(out, w_hi, a_lo, start=False, stop=False)
                ins = pe.matmul(out, w_hi, a_hi, start=False, stop=k == 1)
        ins.then_inc(M.used[j], 1)

    o = job["pool_o"]
    panel(o, 0, acts=M.mk["pool_o"])
    with pe.Fori(0, o.n - 1) as i:
        panel(o, i + 1)
    o = job["out2"]
    panel(o, 0, acts=M.mk["out2"])
    with pe.Fori(0, o.n - 1) as i:
        panel(o, i + 1)

    live_sums(34)
    for k in range(DC):
        pe.wait_ge(M.sq_done, 33 + k)
        ins = pe.matmul(M.X[:, 512:512 + LIVE], ones[:, 0:P], M.sqr[:, (k % 4) * ROWS:(k % 4) * ROWS + LIVE],
                        start=k == 0, stop=k == DC - 1)
        ins.then_inc(M.xsum, 1)

    def stream_rows(n):
        def go():
            t, c = n // 4, n % 4
            if n < 2:
                pe.wait_ge(M.rs_ready, 13)
            else:
                pe.wait_ge(M.rr_done, n - 1)
            for k in range(4):
                src = M.rT[:, (4 * c + k) * ROWS + META + t * P:(4 * c + k) * ROWS + META + (t + 1) * P]
                ins = transpose(M.X[:, (n % 2) * 512 + k * P:(n % 2) * 512 + (k + 1) * P], src)
            ins.then_inc(M.rr_t, 1)
        return go

    up = job["up"]
    panel(up, 0, acts=M.mk["up"])
    panel(up, 1, {j: [stream_rows(j)] for j in range(8)})
    with pe.Fori(0, up.n // 2 - 1) as i:
        panel(up, 2 * i + 2)
        panel(up, 2 * i + 3)

    down = job["down"]
    banks = [[M.acc[c] for c in range(4)], [M.X[:, 0:512], M.X[:, 512:1024], M.Y[:, 0:512], M.Y[:, 512:1024]]]

    def down_panel(i, first=False, last=False):
        for j in range(down.J):
            s, kk, half = j % SLOTS, j // 2, j % 2
            pe.wait_ge(M.lo_ready[s], down.raw0 + down.turn(i, j) + 1)
            pe.wait_ge(M.dl_ready, 4 * i + kk + 1)
            for t in range(2):
                for e in range(2):
                    cb = 2 * half + e
                    out = banks[t][cb][:, 0:512]
                    start, stop = first and kk == 0, last and kk == 3
                    if start and t == 0:
                        pe.wait_ge(M.acc_free[cb], down.free0[cb])
                    if start and t == 1 and cb == 0:
                        pe.wait_ge(M.rr_done, 8)
                    at = kk * SEQ + t * P
                    d_hi, d_lo = M.d_hi[:, at:at + P], M.d_lo[:, at:at + P]
                    w_hi, w_lo = M.hi[s][:, e * 512:(e + 1) * 512], M.lo[s][:, e * 512:(e + 1) * 512]
                    pe.matmul(out, d_lo, w_hi, start=start, stop=False)
                    pe.matmul(out, d_hi, w_lo, start=False, stop=False)
                    ins = pe.matmul(out, d_hi, w_hi, start=False, stop=stop)
            ins.then_inc(M.down_done if last and j == down.J - 1 else M.used[s], 1)

    down_panel(0, first=True)
    with pe.Fori(0, down.n - 2) as i:
        down_panel(i + 1)
    down_panel(down.n - 1, last=True)


def sum_x(M, pe, k):
    pe.wait_ge(M.xt_done, k + 1)
    ins = pe.matmul(M.X[:, 512:512 + SEQ], M.ones[:, 0:P], M.sq[:, (k % 4) * SEQ:(k % 4 + 1) * SEQ],
                    start=k == 0, stop=k == DC - 1)
    ins.then_inc(M.xsum, 1)


def act_program(M, act):
    A, job = M.A, M.job
    ch = Chain(act, M.chain_a)

    def table(n):
        act.add_instruction(mybir.InstLoadActFuncSet(
            name=M.nc.get_next_instruction_name(), act_func_set_id=n,
            engine=mybir.EngineType.Activation, ins=[], outs=[]))

    def split(job, i, j):
        s = j % SLOTS
        act.wait_ge(M.raw_in[s], 16 * (job.raw0 + job.turn(i, j) + 1))
        at_least(act, M.used[s], job.used0[s] + (job.normal(i, j) if s == 3 else job.turn(i, j)))
        if j == 3:
            at_least(act, M.acc_ready[3], job.ready0[3] + (0 if job.name in ("pool_w", "down") else i))
        act.activation(M.hi[s][:, 0:job.width], M.raw[s][:, 0:job.width], ACT.Copy).then_inc(M.hi_ready[s], 1)

    def panel(job, i, after={}, before={}):
        for j in range(job.J):
            for step in before.get(j, ()):
                step()
            split(job, i, j)
            for step in after.get(j, ()):
                step()

    def rstd(sem, count, src, dst, tmp, n, rows=P):
        act.wait_ge(sem, count)
        ch.step(act.activation(dst, src, ACT.Ln, bias=M.eps[0:rows, :], scale=1.0 / n))
        ch.step(act.activation(dst, dst, ACT.Exp, scale=-0.5))
        act.activation(tmp, dst, ACT.Square).then_inc(M.y2_ready, 1)

    def split_acts(name, chunks, src, dst, shift=None, source=0, waits=None, scale=1.0):
        def go():
            for c in chunks:
                if source is not None:
                    act.wait_ge(M.src_ready, source + c + 1)
                if waits is not None:
                    waits(c)
                if shift is None:
                    ins = act.activation(dst(c), src(c), ACT.Copy, scale=scale)
                else:
                    ins = act.activation(dst(c), src(c), ACT.Identity, bias=shift(c))
                ins.then_inc(M.ahi_ready, 1)
        return go

    def spread(J, tail, *args, **kw):
        mk = [split_acts(args[0], (2 * n, 2 * n + 1), *args[1:], **kw) for n in range(J)]
        if J == 4:
            return {2: tail[0], 3: [*tail[1], *mk]}
        return {2: tail[0], 3: [*tail[1], mk[0], mk[1]], 4: [mk[2]], 5: [mk[3]], 6: [mk[4]],
                7: [mk[5], mk[6], mk[7]]}

    x = A["x"].rearrange("a (t p) d -> p (a t) d", p=P)
    for t in range(2):
        act.dma_start(M.x_rows[:, t * D:(t + 1) * D], x[:, t]).then_inc(M.x_in, 16)
    act.dma_start(M.meta_rows[:, :], A["meta_tokens_2"]).then_inc(M.x_in, 16)
    tiles = lambda v: v.rearrange("a (r c) -> (a r) c", c=P)
    for row, n, src in ((V2_PRE, 16, tiles(A["mix_pre_g_2"])), (V2_POST, 16, tiles(A["mix_post_g_2"])),
                        (V2_FFN, 16, tiles(A["ffn_pre_g_2"])), (V2_QKV, 24, tiles(A["b_in_2"][:, 0:3072])),
                        (V2_F, 1, tiles(A["b_in_2"][:, 3072:3200])),
                        (V2_UG, 40, tiles(A["b_in_2"][:, 3080:8200])), (V2_PS, 8, tiles(A["pool_scale_2"]))):
        act.dma_start(M.vec2[row:row + n, :], src).then_inc(M.v_in, 16)
    for t in range(CONV):
        act.dma_start(M.vecc[:, t * P:(t + 1) * P], tiles(A["ffn_conv_w_2"][:, t])).then_inc(M.v_in, 16)
    act.dma_start(M.vecc[:, 3 * P:4 * P], tiles(A["ffn_conv_b_2"])).then_inc(M.v_in, 16)

    act.wait_ge(M.v1_t, 1)
    act.activation(M.c1[:, :], M.Y[:, 0:V1_N], ACT.Copy).then_inc(M.cols, 1)
    act.wait_ge(M.cols, 1)
    act.activation(M.silu_c[:, :], M.c1[:, V1_C:V1_C + DC], ACT.Silu).then_inc(M.silu_c_done, 1)
    for n, (col, f) in enumerate(((V1_QA, HD ** -0.5), (V1_KA, 1.0), (V1_QB, HD ** -0.5), (V1_KB, 1.0))):
        for t in range(2):
            act.activation(M.gqk[:, 2 * n + t:2 * n + t + 1], M.c1[:, col:col + 1], ACT.Copy, scale=f)
    table(TABLE_LN_EXP)
    for k in range(DC):
        act.wait_ge(M.xt_ready, k + 1)
        if k >= 4:
            act.wait_ge(M.xsum, k - 3)
        act.activation(M.rT[:, k * ROWS:(k + 1) * ROWS], M.acc[k % 4][:, 0:ROWS], ACT.Copy)
        act.activation(M.sq[:, (k % 4) * SEQ:(k % 4 + 1) * SEQ], M.acc[k % 4][:, META:ROWS], ACT.Square
                       ).then_inc(M.xt_done, 1)
    rstd(M.xsum, DC, M.X[:, 512:512 + SEQ], M.rs[:, 0:SEQ], M.rs[:, SEQ:2 * SEQ], D)
    act.wait_ge(M.v2_t, 1)
    act.activation(M.c2[:, :], M.Y[:, 512:512 + V2_N], ACT.Copy)
    act.activation(M.cc[:, 3 * CT:4 * CT], M.Y[:, 128:128 + CT], ACT.Copy)
    act.activation(M.cc[:, 0:3 * CT], M.Y[:, 640:640 + 3 * CT], ACT.Copy).then_inc(M.cols, 1)
    act.wait_ge(M.cols, 2)
    act.activation(M.bqkv[:, 0:8], M.c2[:, V2_QKV:V2_QKV + 8], ACT.Copy, scale=HD ** -0.5)
    act.activation(M.bqkv[:, 8:24], M.c2[:, V2_QKV + 8:V2_QKV + 24], ACT.Copy)
    ch.step(act.activation(M.bgate[:, :], M.c2[:, V2_UG + 8:V2_UG + 40], ACT.Copy, scale=0.5), wait=False)

    def hi_of(k, c0=0, n=SEQ):
        return M.act_hi[:, ROWS * k + c0:ROWS * k + c0 + n]

    def stored(job, i, tile, func=ACT.Copy, squares=None):
        def go():
            for m in range(4):
                act.wait_ge(M.acc_ready[m], job.ready0[m] + i + 1)
                dst = M.store[:, ds((tile + m) * SEQ if isinstance(tile, int) else (tile * SEQ + m * SEQ), SEQ)]
                ins = act.activation(dst, M.acc[m][:, 0:SEQ], func)
                if squares is not None:
                    if m == 0:
                        act.wait_ge(M.rs_ready, squares)
                    ins = act.activation(M.sq[:, m * SEQ:(m + 1) * SEQ], M.acc[m][:, 0:SEQ], ACT.Square)
                ins.then_inc(M.acc_free[m], 1)
        return go

    q0, strip, q1 = job["qidx0"], job["strip"], job["qidx1"]
    panel(q0, 0, spread(8, ((), ()), "qidx0", lambda c: M.sq[:, (c % 4) * SEQ:(c % 4 + 1) * SEQ],
                        hi_of, shift=lambda c: M.shift[:, c:c + 1], source=0))
    panel(strip, 0, {2: [stored(q0, 0, 0)]})

    def strip_stored():
        act.wait_ge(M.acc_ready[3], strip.ready0[3] + 1)
        act.activation(M.kst[:, :], M.acc[3][:, 0:SEQ], ACT.Copy)
        act.activation(M.sq[0:IDX_DIM, 0:SEQ], M.acc[3][0:IDX_DIM, 0:SEQ], ACT.Square
                       ).then_inc(M.acc_free[3], 1)

    def k_idx_rstd():
        rstd(M.ss_ready, 1, M.Y[0:IDX_DIM, 0:SEQ], M.rs[0:IDX_DIM, 0:SEQ], M.rs[0:IDX_DIM, SEQ:2 * SEQ],
             IDX_DIM, IDX_DIM)

    def k_idx_store():
        act.wait_ge(M.kd_ready, 1)
        act.activation(M.k_idx[:, :], M.X[:, 512:512 + SEQ], ACT.Copy).then_inc(M.kidx_ready, 1)

    panel(q1, 0, {2: [strip_stored], 4: [k_idx_rstd]})

    def qk_rstd(ss, before):
        def go():
            act.wait_ge(M.norm_done, before + 1)
            rstd(M.ss_ready, ss, M.Y[:, :], M.rs[:, :], M.sq[:, :], HD)
        return go

    def relus(n):
        def go():
            act.wait_ge(M.il_ready, n + 1)
            at_least(act, M.rl_used, n)
            act.activation(M.relu[:, :].rearrange("p (h n) -> p h n", h=2),
                           M.X[:, :].rearrange("p (h n) -> p h n", h=2)[:, :, 0:384], ACT.Relu,
                           scale=IDX_DIM ** -0.5).then_inc(M.rl_ready, 1)
        return go

    a, b = job["qk_a"], job["qk_b"]
    panel(a, 0, {1: [k_idx_store], 2: [stored(q1, 0, 4)], 4: [relus(0)], 7: [relus(1)]})
    with act.Fori(0, a.n - 1) as i:
        ch.enter(i, 2)
        panel(a, i + 1, {2: [stored(a, i, 8 + i * 4, squares=i + 2)], 4: [qk_rstd(i + 2, i)],
                         5: [relus(2 * i + 2)], 7: [relus(2 * i + 3)]})
        ch.leave(a.n - 1)
    panel(job["v_a"], 0, {2: [stored(a, 3, 20, squares=5)], 4: [qk_rstd(5, 3)]})
    panel(job["v_a"], 1, {2: [stored(job["v_a"], 0, 24)]})

    def exps(u):
        def go():
            act.wait_ge(M.nm_ready, u + 1)
            for h in range(2):
                for t in range(2):
                    part = M.prob[:, h * 384 + t * P:h * 384 + t * P + (t + 1) * P]
                    n = 2 * h + t
                    ins = act.activation(part, part, ACT.Exp, bias=M.nmax[:, n:n + 1],
                                         accum_out=M.sums[:, n:n + 1])
            ins.then_inc(M.e_ready, 1)
        return go

    def probs_a(u):
        def go():
            act.wait_ge(M.pt_ready, u + 1)
            at_least(act, M.o_ready, u)
            act.activation(M.probT[:, 0:384], M.X[:, 0:384], ACT.Copy).then_inc(M.pt_a, 1)
        return go

    def out_stored(u, at):
        def go():
            act.wait_ge(M.o_ready, u + 1)
            act.activation(M.store[:, ds(at, 512)], M.Y[:, 512:1024], ACT.Copy).then_inc(M.o_done, 1)
        return go

    qa, qb = 8 * SEQ, 32 * SEQ
    panel(b, 0, {2: [stored(job["v_a"], 1, 28)], 5: [exps(0)], 7: [probs_a(0)]})
    with act.Fori(0, b.n - 1) as i:
        ch.enter(i, 2)
        panel(b, i + 1, {2: [out_stored(i, qa + i * 512), stored(b, i, 32 + i * 4, squares=i + 6)],
                         4: [qk_rstd(i + 6, i + 4)], 5: [exps(i + 1)], 7: [probs_a(i + 1)]})
        ch.leave(b.n - 1)
    panel(job["v_b"], 0, {2: [out_stored(3, qa + 3 * 512), stored(b, 3, 44, squares=9)], 4: [qk_rstd(9, 7)]})
    panel(job["v_b"], 1, {2: [stored(job["v_b"], 0, 48)]})
    za, zb = job["z_a"], job["z_b"]
    panel(za, 0, {2: [stored(job["v_b"], 1, 52)], 5: [exps(4)], 7: [probs_a(4)]})
    panel(za, 1, {2: [out_stored(4, qb), stored(za, 0, 0, ACT.Silu)], 5: [exps(5)], 7: [probs_a(5)]})
    panel(zb, 0, {2: [out_stored(5, qb + 512), stored(za, 1, 4, ACT.Silu)], 5: [exps(6)], 7: [probs_a(6)]})
    panel(zb, 1, {2: [out_stored(6, qb + 1024), stored(zb, 0, 24, ACT.Silu)], 5: [exps(7)], 7: [probs_a(7)]})

    oa, ob = job["out_a"], job["out_b"]
    gated = lambda c: M.sq[:, (c % 4) * SEQ:(c % 4 + 1) * SEQ]
    panel(oa, 0, spread(4, ([out_stored(7, qb + 1536), stored(zb, 1, 28, ACT.Silu)], ()), "out_a", gated,
                        lambda c: M.ya_hi[:, SEQ * c:SEQ * (c + 1)], source=16))
    with act.Fori(0, oa.n - 1) as i:
        panel(oa, i + 1)
    panel(ob, 0, spread(4, ((), ()), "out_b", gated, hi_of, source=24))

    def stream_squares(base, i):
        def go():
            for m in range(4):
                act.wait_ge(M.acc_free[m], job["out_b"].free0[m] + i + 1)
                n = base + 4 * i + m
                if not isinstance(i, int) or n >= 4:
                    act.wait_ge(M.ssum_done, n - 2)
                src = M.rT[:, ds((4 * i + m) * ROWS, ROWS)]
                act.activation(M.sqr[:, m * ROWS:(m + 1) * ROWS], src, ACT.Square).then_inc(M.sq_done, 1)
        return go

    panel(ob, 1, {2: [stream_squares(0, 0)]})
    with act.Fori(0, ob.n - 2) as i:
        panel(ob, i + 2, {2: [stream_squares(0, i + 1)]})

    qkv, f2, u2, g2 = job["qkv2"], job["f2"], job["u2"], job["g2"]

    def live_rstd(sem, count, src, c0, n):
        def go():
            table(TABLE_LN_EXP)
            rstd(sem, count, src, M.rs2[:, c0:c0 + n], M.tmp2[:, c0:c0 + n], D)
        return go

    ht = lambda n: (lambda c: M.ht[:, (c % 4) * ROWS:(c % 4) * ROWS + n])
    panel(qkv, 0, spread(8, ([stream_squares(0, 3)], [live_rstd(M.ss_ready, 10, M.X[:, 0:ROWS], 0, ROWS)]),
                         "qkv2", ht(ROWS), lambda c: hi_of(c, 0, ROWS), source=32))

    def biased(job, i, n, dst, bias, scale=1.0, func=ACT.Identity):
        def go():
            for m in range(4):
                act.wait_ge(M.acc_ready[m], job.ready0[m] + i + 1)
                act.activation(dst(m), M.acc[m][:, 0:n], func, bias=bias(m), scale=scale
                               ).then_inc(M.acc_free[m], 1)
        return go

    def qkv_stored(i):
        return biased(qkv, i, ROWS, lambda m: M.qkv[:, ds(i * 4 * ROWS + m * ROWS, ROWS)],
                      lambda m: M.bqkv[:, ds(i * 4 + m, 1)], M.qsc[:, ds(i, 1)])

    with act.Fori(0, qkv.n - 1) as i:
        panel(qkv, i + 1, {2: [qkv_stored(i)]})
    panel(f2, 0, {2: [qkv_stored(qkv.n - 1)]})

    def f_stored():
        act.wait_ge(M.acc_ready[3], f2.ready0[3] + 1)
        act.activation(M.fx[:, 0:ROWS], M.acc[3][0:HEADS, 0:ROWS], ACT.Identity,
                       bias=M.c2[0:HEADS, V2_F:V2_F + 1]).then_inc(M.acc_free[3], 1)

    def f_logs():
        act.wait_ge(M.acc_free[3], f2.free0[3] + 1)
        t = M.tmp2[0:HEADS, :]
        ch.step(act.activation(t, M.fx[:, 0:ROWS], ACT.Abs))
        ch.step(act.activation(t, t, ACT.Exp, scale=-1.0))
        act.activation(t, t, ACT.Ln, bias=M.ones[0:HEADS, 0:1]).then_inc(M.f_ln, 1)

    def u_stored(i):
        return biased(u2, i, ROWS, lambda m: M.u[:, (4 * i + m) * ROWS:(4 * i + m + 1) * ROWS],
                      lambda m: M.c2[:, V2_UG + 4 * i + m:V2_UG + 4 * i + m + 1])

    def gates_stored(i):
        return biased(g2, i, LIVE, lambda m: M.G[:, ds(i * 4 * LIVE + m * LIVE, LIVE)],
                      lambda m: M.bgate[:, ds(i * 4 + m, 1)], 0.5, ACT.Tanh)

    panel(u2, 0, {2: [f_stored, f_logs]})
    panel(u2, 1, {2: [u_stored(0)]})

    tiles2 = ((0, 144, P), (144, ROWS, P), (416, ROWS, 2))

    def exps2(h):
        def go():
            act.wait_ge(M.nm2_ready, h + 1)
            for t, (c0, n, rows) in enumerate(tiles2):
                part = M.prob2[0:rows, c0:c0 + n]
                ins = act.activation(part, part, ACT.Exp, bias=M.nmax[0:rows, t:t + 1],
                                     accum_out=M.sums[0:rows, t:t + 1])
            ins.then_inc(M.e2_ready, 1)
        return go

    def probs_a2(h):
        def go():
            act.wait_ge(M.pt2_ready, h + 1)
            at_least(act, M.o2_ready, h)
            act.activation(M.probT2[:, 0:LIVE], M.X[:, 0:LIVE], ACT.Copy)
            act.activation(M.probT2[0:16, 2 * LIVE:2 * LIVE + 130], M.X[0:16, LIVE:LIVE + 130], ACT.Copy
                           ).then_inc(M.pt2_a, 1)
        return go

    def out2_stored(h):
        def go():
            act.wait_ge(M.o2_ready, h + 1)
            act.activation(M.qkv[:, ds(h * ROWS, LIVE)], M.Y[:, 512:512 + LIVE], ACT.Copy
                           ).then_inc(M.o2_done, 1)
        return go

    table(TABLE_EXP_TANH)
    panel(g2, 0, {2: [u_stored(1)], 5: [exps2(0)], 7: [probs_a2(0)]})
    with act.Fori(0, g2.n - 1) as i:
        panel(g2, i + 1, {2: [out2_stored(i), gates_stored(i)], 5: [exps2(i + 1)], 7: [probs_a2(i + 1)]})

    ao, pw, po, o2 = job["attn_o"], job["pool_w"], job["pool_o"], job["out2"]

    def o_done(c):
        act.wait_ge(M.o2_done, HEADS)

    panel(ao, 0, spread(4, ([out2_stored(7), gates_stored(7)], ()), "attn_o",
                        lambda c: M.qkv[:, c * ROWS:c * ROWS + LIVE],
                        lambda c: M.o_hi[:, c * LIVE:(c + 1) * LIVE], source=None, waits=o_done))
    with act.Fori(0, ao.n - 1) as i:
        panel(ao, i + 1)

    def d_done(c):
        act.wait_ge(M.d_done, c // 2 + 1)

    yp = M.qkv[:, 0:8 * ROWS]

    def pooled_stored(n):
        def go():
            act.wait_ge(M.used[n], pw.used0[n] + 1)
            for e in range(2):
                m = 2 * n + e
                act.activation(yp[:, m * ROWS:m * ROWS + LIVE], M.acc[m % 4][:, 0:LIVE], ACT.Copy,
                               scale=M.c2[:, V2_PS + m:V2_PS + m + 1]).then_inc(M.acc_free[m % 4], 1)
        return go

    panel(pw, 0, {3: [split_acts("pool_w", range(8), lambda c: M.u[:, c * ROWS + LIVE0:(c + 1) * ROWS],
                                 lambda c: hi_of(c, 0, LIVE), source=None, waits=d_done)]
                  + [pooled_stored(n) for n in range(4)]})

    def yp_done(c):
        act.wait_ge(M.acc_free[c % 4], pw.free0[c % 4] + c // 4 + 1)

    panel(po, 0, spread(4, ((), ()), "pool_o", lambda c: yp[:, c * ROWS:c * ROWS + LIVE],
                        lambda c: hi_of(8 + c, 0, LIVE), source=None, waits=yp_done))
    with act.Fori(0, po.n - 1) as i:
        panel(po, i + 1)

    def m_done(c):
        act.wait_ge(M.m_sum, c + 1)
        if c >= 8:
            act.wait_ge(M.m_sum, 16)

    panel(o2, 0, spread(8, ((), ()), "out2", lambda c: M.G[:, c * LIVE:(c + 1) * LIVE],
                        lambda c: hi_of(c, 0, LIVE), source=None, waits=m_done, scale=0.5))

    def mixed_stored(i):
        def go():
            for m in range(4):
                act.wait_ge(M.acc_ready[m], o2.ready0[m] + i + 1)
                act.activation(M.G[:, ds((16 + 4 * i + m) * LIVE if isinstance(i, int) else
                                         i * 4 * LIVE + (16 + m) * LIVE, LIVE)], M.acc[m][:, 0:LIVE], ACT.Copy)
                act.wait_ge(M.ssum_done, 4 * i + m + 15)
                ins = act.activation(M.sqr[:, m * ROWS + LIVE0:(m + 1) * ROWS], M.acc[m][:, 0:LIVE], ACT.Square)
                ins.then_inc(M.acc_free[m], 1)
                act.wait_ge(M.acc_free[m], o2.free0[m] + i + 1)
                act.sem_inc(M.sq_done, 1)
        return go

    with act.Fori(0, o2.n - 1) as i:
        panel(o2, i + 1, {2: [mixed_stored(i)]})

    up, down = job["up"], job["down"]

    def new_squares():
        for c in range(DC):
            act.wait_ge(M.r_upd, c + 1)
            if c >= 4:
                act.wait_ge(M.xsum, DC + c - 3)
            act.activation(M.sqr[:, (c % 4) * ROWS:(c % 4) * ROWS + LIVE],
                           M.rT[:, c * ROWS + LIVE0:(c + 1) * ROWS], ACT.Square).then_inc(M.sq_done, 1)

    panel(up, 0, spread(8, ([mixed_stored(3)],
                            [live_rstd(M.ss_ready, 11, M.X[:, LIVE0:ROWS], LIVE0, LIVE), new_squares,
                             live_rstd(M.xsum, 2 * DC, M.X[:, 512:512 + LIVE], LIVE0, LIVE)]),
                        "up", ht(LIVE), lambda c: hi_of(c, 0, LIVE), source=48))

    def conv_first(i, part, dst):
        def go():
            if part == 0:
                at_least(act, M.gg_ready, i)
            else:
                at_least(act, M.F_ready, i)
            for m in range(4):
                act.wait_ge(M.acc_ready[m], up.ready0[m] + 2 * i + part + 1)
                tile = i * 4 + (part * FC + m)
                act.activation(dst[:, m * SEQ:(m + 1) * SEQ], M.acc[m][:, CONV - 1:LIVE], ACT.Identity,
                               scale=M.cc[:, ds(tile + 2 * CT, 1)], bias=M.cc[:, ds(tile + 3 * CT, 1)]
                               ).then_inc(M.cv_ready, 1)
        return go

    def gelu(i):
        def go():
            act.wait_ge(M.acc_free[3], up.free0[3] + 2 * i + 1)
            at_least(act, M.F_ready, i)
            act.activation(M.gg[:, :], M.gt[:, :], ACT.Gelu_apprx_tanh).then_inc(M.gg_ready, 1)
        return go

    def rows_stored(n):
        def go():
            act.wait_ge(M.rr_t, n + 1)
            act.activation(M.r_rows[:, n * 512:(n + 1) * 512], M.X[:, (n % 2) * 512:(n % 2 + 1) * 512], ACT.Copy
                           ).then_inc(M.rr_done, 1)
        return go

    panel(up, 1, {2: [conv_first(0, 0, M.gt)], 3: [gelu(0)], 4: [rows_stored(0)],
                  5: [rows_stored(1)], 6: [rows_stored(2)], 7: [rows_stored(3)]})
    rest = {0: [rows_stored(4)], 1: [rows_stored(5), rows_stored(6)], 2: [conv_first(0, 1, M.vt), rows_stored(7)]}
    panel(up, 2, rest)
    panel(up, 3, {2: [conv_first(1, 0, M.gt)], 3: [gelu(1)]})
    with act.Fori(0, up.n // 2 - 2) as i:
        panel(up, 2 * i + 4, {2: [conv_first(i + 1, 1, M.vt)]})
        panel(up, 2 * i + 5, {2: [conv_first(i + 2, 0, M.gt)], 3: [gelu(i + 2)]})

    def down_act(i, kk):
        def go():
            act.wait_ge(M.F_ready, i + 1)
            at_least(act, M.used[(2 * kk + 1) % 4],
                     0 if isinstance(i, int) and i == 0 else
                     down.used0[(2 * kk + 1) % 4] + 2 * i - 1 + kk // 2)
            act.activation(M.d_hi[:, kk * SEQ:(kk + 1) * SEQ], M.F[:, ds(i * 4 * SEQ + kk * SEQ, SEQ)], ACT.Copy
                           ).then_inc(M.dh_ready, 1)
        return go

    mk = lambda i: {2 * kk: [down_act(i, kk)] for kk in range(4)}
    panel(down, 0, {2: [conv_first(10, 1, M.vt)]}, mk(0))
    with act.Fori(0, down.n - 1) as i:
        panel(down, i + 1, {}, mk(i + 1))

    act.wait_ge(M.down_done, 1)
    table(TABLE_LN_EXP)
    for n in range(8):
        t, c = n // 4, n % 4
        bank = M.acc[c][:, 0:512] if t == 0 else (M.X, M.X, M.Y, M.Y)[c][:, (c % 2) * 512:(c % 2 + 1) * 512]
        ins = act.activation(M.F[:, n * 512:(n + 1) * 512], bank, ACT.Square, accum_out=M.ss8[:, n:n + 1])
    ins.then_inc(M.fin_ss, 1)
    act.wait_ge(M.fin_v, 1)
    ch.step(act.activation(M.rsf[:, 2:4], M.rsf[:, 0:2], ACT.Ln))
    ch.step(act.activation(M.rsf[:, 2:4], M.rsf[:, 2:4], ACT.Exp, scale=-0.5))
    act.activation(M.rsf[:, 4:6], M.rsf[:, 2:4], ACT.Square).then_inc(M.fin_ls, 1)


def dve_program(M, dve):
    job = M.job
    ch = Chain(dve, M.chain_v)
    store = M.store

    def stt(out, in0, scalar, in1, op0, op1):
        return dve.scalar_tensor_tensor(out, in0, scalar, in1, op0, op1)

    def split(job, i, j):
        s = j % SLOTS
        dve.wait_ge(M.hi_ready[s], job.hi0 + job.turn(i, j) + 1)
        dve.tensor_tensor(M.lo[s][:, 0:job.width], M.raw[s][:, 0:job.width],
                          M.hi[s][:, 0:job.width].bitcast(FP32), ALU.subtract).then_inc(M.lo_ready[s], 1)

    def panel(job, i, after={}, before={}):
        for j in range(job.J):
            for step in before.get(j, ()):
                step()
            split(job, i, j)
            for step in after.get(j, ()):
                step()

    def refine(count, n, src, dst, tmp):
        dve.wait_ge(M.y2_ready, count)
        ch.step(stt(tmp, src, n * EPS, tmp, ALU.add, ALU.mult))
        ch.step(dve.tensor_scalar(tmp, tmp, -0.5 / n, 1.5, ALU.mult, ALU.add))
        dve.tensor_tensor(dst, dst, tmp, ALU.mult).then_inc(M.rs_ready, 1)
        dve.wait_ge(M.rs_ready, count)

    def spread(J, tail, name, make, low):
        n_chunks = 2 * J

        def mk(n):
            def go():
                ahead = (0, 1, 2, 3) if n == 0 else (2 * n + 2, 2 * n + 3)
                if make is not None:
                    for c in ahead:
                        if 4 <= c < n_chunks:
                            dve.wait_ge(M.act_ready, M.mk[name] + c - 3)
                        if c < n_chunks:
                            make(c)
                for c in (2 * n, 2 * n + 1):
                    dve.wait_ge(M.ahi_ready, M.mk[name] + c + 1)
                    low(c).then_inc(M.act_ready, 1)
            return go
        steps = [mk(n) for n in range(J)]
        if J == 4:
            return {2: tail[0], 3: [*tail[1], *steps]}
        return {2: tail[0], 3: [*tail[1], steps[0], steps[1]], 4: [steps[2]], 5: [steps[3]], 6: [steps[4]],
                7: [steps[5], steps[6], steps[7]]}

    sq = lambda c: M.sq[:, (c % 4) * SEQ:(c % 4 + 1) * SEQ]
    part_hi = lambda k, n=SEQ: M.act_hi[:, ROWS * k:ROWS * k + n].bitcast(FP32)
    part_lo = lambda k, n=SEQ: M.act_lo[:, ROWS * k:ROWS * k + n]

    dve.wait_ge(M.consts, 1)
    dve.wait_ge(M.silu_c_done, 1)
    for t in range(2):
        def rows_summed(i):
            for s in range(SLOTS):
                dve.wait_ge(M.raw_in[s], 16 * (i + t * (DC // 2) + 1))
                at_least(dve, M.lo_ready[(s - 2) % 4], i + t * (DC // 2) + s // 2)
                half = M.ada_acc[:, (s % 2) * PIECE:(s % 2 + 1) * PIECE]
                stt(half, M.raw[s][:, :], M.silu_c[:, ds(2 * i + s // 2, 1)], half, ALU.mult, ALU.add
                    ).then_inc(M.lo_ready[s], 1)

        rows_summed(0)
        with dve.Fori(0, DC // 2 - 1) as i:
            rows_summed(i + 1)
        dve.wait_ge(M.ada_cols, t + 1)
        ch.step(dve.memset(M.ada_acc[:, :], 0.0))
    dve.wait_ge(M.cols, 1)
    ch.step(dve.tensor_tensor(M.shift[:, :], M.X[:, 0:DC], M.c1[:, V1_BADA:V1_BADA + DC], ALU.add), wait=False)
    ch.step(dve.tensor_tensor(M.gs[:, :], M.X[:, DC:2 * DC], M.c1[:, V1_BADA + DC:V1_BADA + 2 * DC], ALU.add))
    ch.step(stt(M.gs[:, :], M.gs[:, :], 1.0, M.c1[:, V1_G:V1_G + DC], ALU.add, ALU.mult))
    refine(1, D, M.X[:, 512:512 + SEQ], M.rs[:, 0:SEQ], M.rs[:, SEQ:2 * SEQ])

    def gate_sum(b, turn, k, waited=False):
        def go():
            dve.wait_ge(M.ada_in[b], 16 * (turn + 1))
            at_least(dve, M.ada_used[1 - b], turn + b)
            stt(M.ada_acc[:, :], M.ada_x[b][:, :], M.silu_c[:, ds(k, 1)], M.ada_acc[:, :], ALU.mult, ALU.add
                ).then_inc(M.ada_used[b], 1)
        return go

    def h_chunk(c):
        stt(sq(c), M.rT[:, c * ROWS + META:(c + 1) * ROWS], M.gs[:, c:c + 1], M.rs[:, 0:SEQ],
            ALU.mult, ALU.mult).then_inc(M.src_ready, 1)

    panel(job["qidx0"], 0, spread(8, ((), ()), "qidx0", h_chunk, lambda c: stt(
        part_lo(c), sq(c), M.shift[:, c:c + 1], part_hi(c), ALU.add, ALU.subtract)))
    panel(job["strip"], 0)

    def k_idx():
        dve.wait_ge(M.kw_ready, 1)
        for t in range(2):
            dve.tensor_scalar(M.w_idx[:, t * IDX_HEADS:(t + 1) * IDX_HEADS],
                              M.X[:, t * P + IDX_DIM:t * P + IDX_DIM + IDX_HEADS],
                              IDX_HEADS ** -0.5, 0.0, ALU.mult, ALU.add)
        r = slice(0, IDX_DIM)
        refine(2, IDX_DIM, M.Y[r, 0:SEQ], M.rs[r, 0:SEQ], M.rs[r, SEQ:2 * SEQ])
        stt(M.knn[:, :], M.kst[r, :], M.c1[r, V1_KI:V1_KI + 1], M.rs[r, 0:SEQ], ALU.mult, ALU.mult
            ).then_inc(M.norm_done, 1)

    panel(job["qidx1"], 0, {3: [gate_sum(0, 0, 0)], 5: [k_idx], 6: [gate_sum(1, 0, 1)]})

    def qk_norm(count, at, gain):
        def go():
            refine(count, HD, M.Y[:, :], M.rs[:, :], M.sq[:, :])
            part = store[:, ds(at, 4 * SEQ)]
            stt(part, part, M.gqk[:, ds(gain, 1)], M.rs[:, :], ALU.mult, ALU.mult).then_inc(M.norm_done, 1)
        return go

    def index_sum(u, tile, first=False):
        def go():
            if first:
                dve.wait_ge(M.score_zero, 1)
            dve.wait_ge(M.rl_ready, 2 * u + tile + 1)
            for half in range(2):
                ch.wait()
                for t in range(2):
                    n = (t + 1) * P
                    part = M.idx_score[:, t * P:t * P + n]
                    col = t * IDX_HEADS + 2 * tile + half
                    ins = stt(part, M.relu[:, half * 384 + t * P:half * 384 + t * P + n],
                              M.w_idx[:, ds(4 * u + col, 1)], part, ALU.mult, ALU.add)
                    if half == 0 or t == 0:
                        ch.step(ins, wait=False)
                    else:
                        ins.then_inc(M.rl_used, 1)
            dve.wait_ge(M.rl_used, 2 * u + tile + 1)
        return go

    a, b = job["qk_a"], job["qk_b"]
    panel(a, 0, {3: [gate_sum(0, 1, 2)], 5: [index_sum(0, 0, True)], 6: [gate_sum(1, 1, 3)],
                 7: [index_sum(0, 1)]})
    with dve.Fori(0, a.n - 1) as i:
        ch.enter(i, 8)
        panel(a, i + 1, {3: [gate_sum(0, i + 2, 2 * i + 4)],
                         5: [index_sum(i + 1, 0), qk_norm(i + 3, (i + 2) * 4 * SEQ, i)],
                         6: [gate_sum(1, i + 2, 2 * i + 5)], 7: [index_sum(i + 1, 1)]})
        ch.leave(a.n - 1)

    def candidates():
        ch.step(dve.tensor_scalar(M.work[:, :], M.dist[:, :], NEG / 10, NEG, ALU.is_lt, ALU.mult))
        ch.step(dve.tensor_tensor(M.work[:, :], M.work[:, :], M.idx_score[:, :], ALU.add))

    def pick():
        for t in range(2):
            part = M.work[:, t * P:t * P + (t + 1) * P]
            ch.step(dve.max(M.max8[:, 8 * t:8 * t + 8], part))
            ch.step(dve.match_replace(part, M.max8[:, 8 * t:8 * t + 8], part, SENTINEL))

    def selected():
        ch.step(dve.tensor_scalar(M.work[:, :], M.work[:, :], SENTINEL / 2, NEG, ALU.is_gt, ALU.mult))
        ch.step(dve.tensor_tensor(M.dist_sel[:, :], M.work[:, :], M.dist[:, :], ALU.add))

    panel(job["v_a"], 0, {1: [candidates, pick], 3: [pick], 5: [qk_norm(6, 20 * SEQ, 3), pick], 7: [pick]})
    panel(job["v_a"], 1, {1: [pick], 3: [pick], 5: [pick], 7: [pick, selected]})

    def hooks(u, head, dist, extra=()):
        def softmax_in():
            dve.wait_ge(M.s_ready, u + 1)
            at_least(dve, M.pt_ready, u)
            for h in range(2):
                ch.step(stt(M.prob[:, h * 384:(h + 1) * 384], dist[:, :], M.slopes[:, ds(head + h, 1)],
                            M.X[:, h * 512:h * 512 + 384], ALU.mult, ALU.add), wait=False)
            ch.wait()
            for h in range(2):
                for t in range(2):
                    ins = dve.tensor_reduce(M.nmax[:, 2 * h + t:2 * h + t + 1],
                                            M.prob[:, h * 384 + t * P:h * 384 + t * P + (t + 1) * P],
                                            AX.X, ALU.max, negate=True)
            ins.then_inc(M.nm_ready, 1)

        def softmax_out():
            dve.wait_ge(M.e_ready, u + 1)
            ch.step(dve.reciprocal(M.rinv[:, 0:4], M.sums[:, 0:4]))
            for h in range(2):
                for t in range(2):
                    part = M.prob[:, h * 384 + t * P:h * 384 + t * P + (t + 1) * P]
                    ins = dve.tensor_scalar(part, part, M.rinv[:, 2 * h + t:2 * h + t + 1], 0.0, ALU.mult, ALU.add)
            ins.then_inc(M.p_ready, 1)
            dve.wait_ge(M.vt_ready, u + 1)
            at_least(dve, M.o_ready, u)
            dve.tensor_copy(M.v_rows[:, :], M.Y[:, 0:512]).then_inc(M.vr_ready, 1)

        def probs_d():
            dve.wait_ge(M.pt_ready, u + 1)
            at_least(dve, M.o_ready, u)
            dve.tensor_copy(M.probT[:, 384:768], M.X[:, 512:896]).then_inc(M.pt_d, 1)

        return {4: [softmax_in], 5: list(extra), 6: [softmax_out], 7: [probs_d]}

    panel(b, 0, hooks(0, 0, M.dist_sel))
    with dve.Fori(0, b.n - 1) as i:
        ch.enter(i, 5)
        panel(b, i + 1, hooks(i + 1, 2 * i + 2, M.dist_sel, [qk_norm(i + 7, (i + 8) * 4 * SEQ, i + 4)]))
        ch.leave(b.n - 1)

    def gates(n):
        return gate_sum(n % 2, n // 2, n)

    panel(job["v_b"], 0, {1: [gates(10)], 3: [gates(11)], 5: [gates(12), qk_norm(10, 44 * SEQ, 7)]})
    panel(job["v_b"], 1, {1: [gates(13)], 3: [gates(14)], 5: [gates(15)]})

    def gate():
        dve.wait_ge(M.gate_cols, 1)
        dve.tensor_tensor(M.gate[:, :], M.Y[:, 512:512 + DC], M.c1[:, V1_BADA + 2 * DC:V1_BADA + 3 * DC], ALU.add
                          ).then_inc(M.gate_done, 1)

    for u in range(4, 8):
        h = hooks(u, 2 * (u - 4), M.dist)
        if u == 4:
            h[4] = [gate, *h[4]]
        panel(job["z_a" if u < 6 else "z_b"], u % 2, h)

    oa, ob = job["out_a"], job["out_b"]

    def gated(z_tile, o_tile, outputs, zjob):
        def go(c):
            if c == 0:
                dve.wait_ge(M.o_done, outputs)
                dve.wait_ge(M.acc_free[3], zjob.free0[3] + 2)
            dve.tensor_tensor(sq(c), store[:, (o_tile + c) * SEQ:(o_tile + c + 1) * SEQ],
                              store[:, (z_tile + c) * SEQ:(z_tile + c + 1) * SEQ], ALU.mult
                              ).then_inc(M.src_ready, 1)
        return go

    def residual(job, i):
        def go():
            for m in range(4):
                dve.wait_ge(M.acc_ready[m], job.ready0[m] + i + 1)
                part = M.rT[:, ds(4 * i * ROWS + m * ROWS + META, SEQ)]
                stt(part, M.acc[m][:, 0:SEQ], M.gate[:, ds(4 * i + m, 1)], part, ALU.mult, ALU.add
                    ).then_inc(M.acc_free[m], 1)
        return go

    panel(oa, 0, spread(4, ((), ()), "out_a", gated(0, 8, 4, job["z_a"]), lambda c: dve.tensor_tensor(
        M.ya_lo[:, c * SEQ:(c + 1) * SEQ], sq(c), M.ya_hi[:, c * SEQ:(c + 1) * SEQ].bitcast(FP32), ALU.subtract)))
    with dve.Fori(0, oa.n - 1) as i:
        panel(oa, i + 1, {2: [residual(oa, i)]})
    panel(ob, 0, spread(4, ([residual(oa, oa.n - 1)], ()), "out_b", gated(24, 32, 8, job["z_b"]),
                        lambda c: dve.tensor_tensor(part_lo(c), sq(c), part_hi(c), ALU.subtract)))
    with dve.Fori(0, ob.n - 1) as i:
        panel(ob, i + 1, {2: [residual(ob, i)]})

    qkv, f2, u2, g2 = job["qkv2"], job["f2"], job["u2"], job["g2"]
    ht = lambda c, n: M.ht[:, (c % 4) * ROWS:(c % 4) * ROWS + n]

    def stream_rstd():
        refine(11, D, M.X[:, 0:ROWS], M.rs2[:, :], M.tmp2[:, :])

    def h2_chunk(c):
        stt(ht(c, ROWS), M.rT[:, c * ROWS:(c + 1) * ROWS], M.c2[:, V2_PRE + c:V2_PRE + c + 1], M.rs2[:, :],
            ALU.mult, ALU.mult).then_inc(M.src_ready, 1)

    panel(qkv, 0, spread(8, ([residual(ob, ob.n - 1)], [stream_rstd]), "qkv2", h2_chunk,
                         lambda c: dve.tensor_tensor(part_lo(c, ROWS), ht(c, ROWS), part_hi(c, ROWS), ALU.subtract)))
    with dve.Fori(0, qkv.n - 1) as i:
        panel(qkv, i + 1)
    panel(f2, 0)

    def cumulated():
        dve.wait_ge(M.f_ln, 1)
        t = M.tmp2[0:HEADS, :]
        ch.step(stt(t, M.fx[:, 0:ROWS], 0.0, t, ALU.min, ALU.subtract))
        dve.tensor_tensor_scan(M.fx[:, ROWS:2 * ROWS], M.ones[0:HEADS, 0:ROWS], t, 0.0, ALU.mult, ALU.subtract
                               ).then_inc(M.c_ready, 1)

    def c_columns():
        dve.wait_ge(M.cq_t, 1)
        dve.tensor_scalar(M.cq[:, 0:16], M.X[:, 0:16], -1.0, 0.0, ALU.mult, ALU.add)
        dve.tensor_scalar(M.cq[0:2, 16:24], M.X[0:2, 16:24], -1.0, 0.0, ALU.mult, ALU.add).then_inc(M.cq_ready, 1)
        dve.wait_ge(M.cq_ready, 1)

    panel(u2, 0, {4: [cumulated]})
    panel(u2, 1, {7: [c_columns]})

    tiles2 = ((0, 0, 144, P), (144, 144, ROWS, P), (512, 416, ROWS, 2))

    def hooks2(h):
        def softmax_in():
            dve.wait_ge(M.s2_ready, h + 1)
            at_least(dve, M.pt2_ready, h)
            if isinstance(h, int):
                dve.wait_ge(M.masks_done, 1)
            for t, (x, p, n, rows) in enumerate(tiles2):
                ch.step(stt(M.prob2[0:rows, p:p + n], M.X[0:rows, x:x + n], M.cq[0:rows, ds(8 * t + h, 1)],
                            M.mask2[0:rows, p:p + n], ALU.add, ALU.add), wait=False)
            ch.wait()
            for t, (x, p, n, rows) in enumerate(tiles2):
                ins = dve.tensor_reduce(M.nmax[0:rows, t:t + 1], M.prob2[0:rows, p:p + n], AX.X, ALU.max,
                                        negate=True)
            ins.then_inc(M.nm2_ready, 1)

        def softmax_out():
            dve.wait_ge(M.e2_ready, h + 1)
            ch.step(dve.reciprocal(M.rinv[:, 0:3], M.sums[:, 0:3]))
            for t, (x, p, n, rows) in enumerate(tiles2):
                part = M.prob2[0:rows, p:p + n]
                ins = dve.tensor_scalar(part, part, M.rinv[0:rows, t:t + 1], 0.0, ALU.mult, ALU.add)
            ins.then_inc(M.p2_ready, 1)
            dve.wait_ge(M.vt2_ready, h + 1)
            at_least(dve, M.o2_ready, h)
            dve.tensor_copy(M.v_rows2[:, 0:2 * P], M.Y[:, 0:2 * P])
            dve.tensor_copy(M.v_rows2[0:META, 2 * P:3 * P], M.Y[0:META, 2 * P:3 * P]).then_inc(M.vr2_ready, 1)

        def probs_d():
            dve.wait_ge(M.pt2_ready, h + 1)
            at_least(dve, M.o2_ready, h)
            dve.tensor_copy(M.probT2[:, LIVE + P:2 * LIVE], M.X[:, 512 + P:512 + LIVE])
            dve.tensor_copy(M.probT2[0:META, LIVE:LIVE + P], M.X[0:META, 512:512 + P]).then_inc(M.pt2_d, 1)

        return {4: [softmax_in], 6: [softmax_out], 7: [probs_d]}

    panel(g2, 0, hooks2(0))
    with dve.Fori(0, g2.n - 1) as i:
        ch.enter(i, 4)
        panel(g2, i + 1, hooks2(i + 1))
        ch.leave(g2.n - 1)

    ao, pw, po, o2 = job["attn_o"], job["pool_w"], job["pool_o"], job["out2"]

    def times_gate(job, i, tile):
        def go():
            dve.wait_ge(M.acc_free[3], g2.free0[3] + g2.n)
            for m in range(4):
                dve.wait_ge(M.acc_ready[m], job.ready0[m] + i + 1)
                part = M.G[:, ds(4 * i * LIVE + (tile + m) * LIVE, LIVE)]
                stt(part, part, 1.0, M.acc[m][:, 0:LIVE], ALU.add, ALU.mult).then_inc(M.acc_free[m], 1)
        return go

    panel(ao, 0, spread(4, ((), ()), "attn_o", None, lambda c: dve.tensor_tensor(
        M.o_lo[:, c * LIVE:(c + 1) * LIVE], M.qkv[:, c * ROWS:c * ROWS + LIVE],
        M.o_hi[:, c * LIVE:(c + 1) * LIVE].bitcast(FP32), ALU.subtract)))
    with dve.Fori(0, ao.n - 1) as i:
        panel(ao, i + 1, {2: [times_gate(ao, i, 0)]})

    def pooled_low():
        for c in range(8):
            dve.wait_ge(M.ahi_ready, M.mk["pool_w"] + c + 1)
            dve.tensor_tensor(part_lo(c, LIVE), M.u[:, c * ROWS + LIVE0:(c + 1) * ROWS], part_hi(c, LIVE),
                              ALU.subtract).then_inc(M.act_ready, 1)

    panel(pw, 0, {2: [times_gate(ao, ao.n - 1, 0)], 3: [pooled_low]})
    panel(po, 0, spread(4, ((), ()), "pool_o", None, lambda c: dve.tensor_tensor(
        part_lo(8 + c, LIVE), M.qkv[:, c * ROWS:c * ROWS + LIVE], part_hi(8 + c, LIVE), ALU.subtract)))
    with dve.Fori(0, po.n - 1) as i:
        panel(po, i + 1, {2: [times_gate(po, i, 16)]})
    panel(o2, 0, spread(8, ([times_gate(po, po.n - 1, 16)], ()), "out2", None, lambda c: stt(
        part_lo(c, LIVE), M.G[:, c * LIVE:(c + 1) * LIVE], 0.5, part_hi(c, LIVE), ALU.mult, ALU.subtract)))
    with dve.Fori(0, o2.n - 1) as i:
        panel(o2, i + 1)

    live = slice(LIVE0, ROWS)

    def mixer_norm():
        refine(12, D, M.X[:, live], M.rs2[:, live], M.tmp2[:, live])
        for pair in range(DC // 2):
            for c in (2 * pair, 2 * pair + 1):
                ch.step(stt(ht(c, LIVE), M.G[:, (16 + c) * LIVE:(17 + c) * LIVE],
                            M.c2[:, V2_POST + c:V2_POST + c + 1], M.rs2[:, live], ALU.mult, ALU.mult),
                        wait=c % 2 == 1)
            for c in (2 * pair, 2 * pair + 1):
                part = M.rT[:, c * ROWS + LIVE0:(c + 1) * ROWS]
                dve.tensor_tensor(part, part, ht(c, LIVE), ALU.add).then_inc(M.r_upd, 1)
        refine(13, D, M.X[:, 512:512 + LIVE], M.rs2[:, live], M.tmp2[:, live])
        dve.wait_ge(M.r_upd, DC)

    def h3_chunk(c):
        stt(ht(c, LIVE), M.rT[:, c * ROWS + LIVE0:(c + 1) * ROWS], M.c2[:, V2_FFN + c:V2_FFN + c + 1],
            M.rs2[:, live], ALU.mult, ALU.mult).then_inc(M.src_ready, 1)

    up, down = job["up"], job["down"]
    panel(up, 0, spread(8, ((), [mixer_norm]), "up", h3_chunk, lambda c: dve.tensor_tensor(
        part_lo(c, LIVE), ht(c, LIVE), part_hi(c, LIVE), ALU.subtract)))

    def taps(i, part, dst):
        def go():
            for m in range(4):
                dve.wait_ge(M.cv_ready, 8 * i + 4 * part + m + 1)
                tile = 4 * i + (part * FC + m)
                out = dst[:, m * SEQ:(m + 1) * SEQ]
                ch.step(stt(out, M.acc[m][:, 1:1 + SEQ], M.cc[:, ds(tile + CT, 1)], out, ALU.mult, ALU.add))
                stt(out, M.acc[m][:, 0:SEQ], M.cc[:, ds(tile, 1)], out, ALU.mult, ALU.add
                    ).then_inc(M.acc_free[m], 1)
        return go

    panel(up, 1, {2: [taps(0, 0, M.gt)]})
    with dve.Fori(0, up.n // 2 - 1) as i:
        ch.enter(i, 8)
        panel(up, 2 * i + 2, {2: [taps(i, 1, M.vt)]})
        panel(up, 2 * i + 3, {2: [taps(i + 1, 0, M.gt)]})
        ch.leave(up.n // 2 - 1)

    def down_low(i, kk):
        def go():
            dve.wait_ge(M.dh_ready, 4 * i + kk + 1)
            dve.tensor_tensor(M.d_lo[:, kk * SEQ:(kk + 1) * SEQ], M.F[:, ds(i * 4 * SEQ + kk * SEQ, SEQ)],
                              M.d_hi[:, kk * SEQ:(kk + 1) * SEQ].bitcast(FP32), ALU.subtract).then_inc(M.dl_ready, 1)
        return go

    mk = lambda i: {2 * kk: [down_low(i, kk)] for kk in range(4)}
    panel(down, 0, {2: [taps(10, 1, M.vt)]}, mk(0))
    with dve.Fori(0, down.n - 1) as i:
        panel(down, i + 1, {}, mk(i + 1))

    dve.wait_ge(M.fin_ss, 1)
    ch.step(dve.tensor_reduce(M.rsf[:, 0:2], M.ss8[:, :].rearrange("p (t c) -> p t c", t=2), AX.X, ALU.add))
    dve.tensor_scalar(M.rsf[:, 0:2], M.rsf[:, 0:2], 1.0 / D, EPS, ALU.mult, ALU.add).then_inc(M.fin_v, 1)
    dve.wait_ge(M.fin_ls, 1)
    ch.step(dve.tensor_tensor(M.rsf[:, 6:8], M.rsf[:, 0:2], M.rsf[:, 4:6], ALU.mult))
    ch.step(dve.tensor_scalar(M.rsf[:, 6:8], M.rsf[:, 6:8], -0.5, 1.5, ALU.mult, ALU.add))
    ch.step(dve.tensor_tensor(M.rsf[:, 2:4], M.rsf[:, 2:4], M.rsf[:, 6:8], ALU.mult))
    dve.wait_ge(M.g_in, 16)
    dve.wait_ge(M.rr_done, 8)
    for n in range(8):
        t, c = n // 4, n % 4
        bank = M.acc[c][:, 0:512] if t == 0 else (M.X, M.X, M.Y, M.Y)[c][:, (c % 2) * 512:(c % 2 + 1) * 512]
        part = M.y[:, n * 512:(n + 1) * 512]
        stt(part, bank, M.rsf[:, 2 + t:3 + t], M.g_row[:, c * 512:(c + 1) * 512], ALU.mult, ALU.mult
            ).then_inc(M.y_part, 1)
        if n % 2 == 0:
            dve.wait_ge(M.y_part, n + 1)
            dve.tensor_tensor(part, part, M.r_rows[:, n * 512:(n + 1) * 512], ALU.add).then_inc(M.y_even, 1)


def build(nc, A):
    with ExitStack() as ctx:
        M = memory(nc, ctx, A)
        block = ctx.enter_context(nc.Block())

        @block.sync
        def _(sp):
            sp_program(M, sp)

        @block.gpsimd
        def _(pool):
            pool_program(M, pool)

        @block.tensor
        def _(pe):
            pe_program(M, pe)

        @block.scalar
        def _(act):
            act_program(M, act)

        @block.vector
        def _(dve):
            dve_program(M, dve)


NAMES = ("x", "c", "w_ada", "b_ada", "g_norm", "w_in", "q_norm_a", "k_norm_a", "k_norm_idx", "q_norm_b",
         "k_norm_b", "w_out", "meta_tokens_2", "mix_pre_g_2", "w_in_2", "b_in_2", "w_attn_o_2", "pool_w_2",
         "pool_scale_2", "w_pool_o_2", "w_out_2", "mix_post_g_2", "ffn_pre_g_2", "w_ffn_up_2",
         "ffn_conv_w_2", "ffn_conv_b_2", "w_ffn_down_2", "ffn_post_g_2")
MATRICES = ("w_ada", "w_in", "w_out", "w_in_2", "w_attn_o_2", "pool_w_2", "w_pool_o_2", "w_out_2",
            "w_ffn_up_2", "w_ffn_down_2")


def kernel(**inputs):
    import concourse.bacc as _bacc
    from concourse.bass_utils import run_bass_kernel_spmd as _run

    nc = _bacc.Bacc("TRN2", target_bir_lowering=False, num_devices=1)
    arrays, args = {}, {}
    for name in NAMES:
        a = np.ascontiguousarray(inputs[name])
        arrays[f"in_{name}"] = a
        ap = nc.dram_tensor(f"in_{name}", a.shape, FP32, kind="ExternalInput").ap()
        args[name] = ap[0] if name in MATRICES else ap
    args["out"] = nc.dram_tensor("out", (1, SEQ, D), FP32, kind="ExternalOutput").ap()
    build(nc, args)
    r = _run(nc, [arrays], core_ids=[0])
    return r.results[0]["out"]
```
